# Optimizing a Trainium2 kernel written in Bass

```python
import math
import jax, jax.numpy as jnp
from jax import lax
import numpy as np

D_MODEL = 1024
BATCH = 1
SEQ = 128
DEPTH = 2
DEC_BATCH = 1
DEC_SEQ = 512
PAST_LEN = 128

GRID_W = 64
HEAD_DIM = 64
DIFF_HEADS = 4
DIFF_V_DIM = 2 * HEAD_DIM
MLA_HEADS = 8
MLA_Q_RANK = 256
MLA_KV_RANK = 128
MLA_NOPE_DIM = 64
MLA_ROPE_DIM = 32
MLA_QK_DIM = MLA_NOPE_DIM + MLA_ROPE_DIM
MLA_V_DIM = 64
GQA_HEADS = 8
GQA_KV_HEADS = 2
GQA_REP = GQA_HEADS // GQA_KV_HEADS
D_FF = 2816
CONV_WIDTH = 3
ROPE_BASE = 10000.0
NORM_EPS = 1e-6
Q_BLOCK = 128
N_BRANCH = 3

A_WIDTH = DIFF_HEADS * DIFF_V_DIM
B_WIDTH = MLA_HEADS * MLA_V_DIM
C_WIDTH = GQA_HEADS * HEAD_DIM

IN_SIZES = (2 * DIFF_HEADS * HEAD_DIM,
            2 * DIFF_HEADS * HEAD_DIM,
            DIFF_HEADS * DIFF_V_DIM,
            MLA_Q_RANK,
            MLA_KV_RANK + MLA_ROPE_DIM,
            GQA_HEADS * HEAD_DIM,
            GQA_KV_HEADS * HEAD_DIM,
            GQA_KV_HEADS * HEAD_DIM,
            N_BRANCH * D_MODEL)
IN_COLS = sum(IN_SIZES)
IN_SPLITS = tuple(int(s) for s in np.cumsum(IN_SIZES)[:-1])

kernel_name = 'hybrid_diffusion_prefix_step'

def rms_norm(x, g):
    xf = x.astype(jnp.float32)
    y = xf * lax.rsqrt(jnp.mean(xf * xf, axis=-1, keepdims=True) + NORM_EPS)
    return (y * g.astype(jnp.float32)).astype(x.dtype)

def axial_rope_tables(n_tokens, dim):
    rows = n_tokens // GRID_W
    row = jnp.repeat(jnp.arange(rows, dtype=jnp.float32), GRID_W)
    col = jnp.tile(jnp.arange(GRID_W, dtype=jnp.float32), rows)
    quarter = dim // 4
    inv = 1.0 / (ROPE_BASE ** (jnp.arange(quarter, dtype=jnp.float32) / quarter))
    ang = jnp.concatenate([row[:, None] * inv, col[:, None] * inv], axis=-1)
    return jnp.cos(ang), jnp.sin(ang)

def apply_rope(x, cos, sin):
    half = x.shape[-1] // 2
    shape = (x.shape[1],) + (1,) * (x.ndim - 3) + (half,)
    cos = cos.reshape(shape).astype(x.dtype)
    sin = sin.reshape(shape).astype(x.dtype)
    x1, x2 = x[..., :half], x[..., half:]
    return jnp.concatenate([x1 * cos - x2 * sin, x1 * sin + x2 * cos], axis=-1)

def over_query_blocks(fn, q):
    b, t = q.shape[:2]
    nb = t // Q_BLOCK
    blocks = jnp.moveaxis(q.reshape((b, nb, Q_BLOCK) + q.shape[2:]), 1, 0)
    out = jnp.moveaxis(lax.map(fn, blocks), 0, 1)
    return out.reshape((b, t) + out.shape[3:])

def gqa_block(q, k, v):
    scale = q.shape[-1] ** -0.5
    s = jnp.einsum('bqgrd,bsgd->bgrqs', q, k).astype(jnp.float32) * scale
    p = jax.nn.softmax(s, axis=-1).astype(v.dtype)
    return jnp.einsum('bgrqs,bsge->bqgre', p, v)

def diff_block(q, k, v, lam):
    scale = q.shape[-1] ** -0.5
    s = jnp.einsum('bqmhd,bsmhd->bmhqs', q, k).astype(jnp.float32) * scale
    p = jax.nn.softmax(s, axis=-1)
    w = (p[:, 0] - lam * p[:, 1]).astype(v.dtype)
    return jnp.einsum('bhqs,bshe->bqhe', w, v)

def mla_expand(ckv, kpe, p):
    b, s = ckv.shape[:2]
    kv = (rms_norm(ckv, p['mla_kv_norm']) @ p['w_mla_kv_up']).reshape(b, s, MLA_HEADS, MLA_NOPE_DIM + MLA_V_DIM)
    k_nope, v = kv[..., :MLA_NOPE_DIM], kv[..., MLA_NOPE_DIM:]
    k_pe = jnp.broadcast_to(kpe[:, :, None, :], (b, s, MLA_HEADS, MLA_ROPE_DIM))
    k = rms_norm(jnp.concatenate([k_nope, k_pe], axis=-1), p['mla_qk_norm'][1])
    return k, v

def rope_tail(x, cos, sin):
    return jnp.concatenate([x[..., :MLA_NOPE_DIM], apply_rope(x[..., MLA_NOPE_DIM:], cos, sin)], axis=-1)

def token_mixers(h, p, lam_init, rope, ctx):
    b, t, _ = h.shape
    aq, ak, av, bq_d, bkv_d, cq, ck, cv, gates = jnp.split(h @ p['w_in'], IN_SPLITS, axis=-1)
    aq = rms_norm(aq.reshape(b, t, 2, DIFF_HEADS, HEAD_DIM), p['diff_qk_norm'][0])
    ak = rms_norm(ak.reshape(b, t, 2, DIFF_HEADS, HEAD_DIM), p['diff_qk_norm'][1])
    av = av.reshape(b, t, DIFF_HEADS, DIFF_V_DIM)
    bq = (rms_norm(bq_d, p['mla_q_norm']) @ p['w_mla_q_up']).reshape(b, t, MLA_HEADS, MLA_QK_DIM)
    bq = rms_norm(bq, p['mla_qk_norm'][0])
    ckv, kpe = bkv_d[..., :MLA_KV_RANK], bkv_d[..., MLA_KV_RANK:]
    bk, bv = mla_expand(ckv, kpe, p)
    cq = rms_norm(cq.reshape(b, t, GQA_HEADS, HEAD_DIM), p['gqa_qk_norm'][0])
    ck = rms_norm(ck.reshape(b, t, GQA_KV_HEADS, HEAD_DIM), p['gqa_qk_norm'][1])
    cv = cv.reshape(b, t, GQA_KV_HEADS, HEAD_DIM)
    own_ctx = (ak, av, ckv, kpe, ck, cv)

    if rope is not None:
        (cos_h, sin_h), (cos_r, sin_r) = rope
        aq, ak = apply_rope(aq, cos_h, sin_h), apply_rope(ak, cos_h, sin_h)
        bq, bk = rope_tail(bq, cos_r, sin_r), rope_tail(bk, cos_r, sin_r)
        cq, ck = apply_rope(cq, cos_h, sin_h), apply_rope(ck, cos_h, sin_h)
        c_ak, c_av, c_ckv, c_kpe, c_ck, c_cv = ctx
        c_bk, c_bv = mla_expand(c_ckv, c_kpe, p)
        ak = jnp.concatenate([c_ak, ak], axis=1)
        av = jnp.concatenate([c_av, av], axis=1)
        bk = jnp.concatenate([c_bk, bk], axis=1)
        bv = jnp.concatenate([c_bv, bv], axis=1)
        ck = jnp.concatenate([c_ck, ck], axis=1)
        cv = jnp.concatenate([c_cv, cv], axis=1)

    lam_vecs = p['diff_lambda'].astype(jnp.float32)
    lam = (jnp.exp(jnp.sum(lam_vecs[0] * lam_vecs[1])) - jnp.exp(jnp.sum(lam_vecs[2] * lam_vecs[3])) + lam_init)
    oa = over_query_blocks(lambda qb: diff_block(qb, ak, av, lam), aq)
    oa = (rms_norm(oa, p['diff_out_norm']) * (1.0 - lam_init)).reshape(b, t, A_WIDTH)
    ob = over_query_blocks(lambda qb: gqa_block(qb, bk, bv), bq[:, :, :, None, :]).reshape(b, t, B_WIDTH)
    oc = over_query_blocks(lambda qb: gqa_block(qb, ck, cv),
                           cq.reshape(b, t, GQA_KV_HEADS, GQA_REP, HEAD_DIM)).reshape(b, t, C_WIDTH)

    g = jax.nn.sigmoid(gates.reshape(b, t, N_BRANCH, D_MODEL))
    merged = (g[:, :, 0] * (oa @ p['w_branch_a']) + g[:, :, 1] * (ob @ p['w_branch_b'])
              + g[:, :, 2] * (oc @ p['w_branch_c']))
    return merged @ p['w_o'], own_ctx

def conv_ffn(h, p):
    u = h @ p['w_up']
    t = u.shape[1]
    pad = CONV_WIDTH // 2
    up = jnp.pad(u, ((0, 0), (pad, pad), (0, 0)))
    w = p['conv_w']
    u = up[:, 0:t] * w[0] + up[:, 1:t + 1] * w[1] + up[:, 2:t + 2] * w[2] + p['conv_b']
    a, gt = u[..., :D_FF], u[..., D_FF:]
    return (a * jax.nn.silu(gt)) @ p['w_down']

def trunk_layer(x, mod, p, lam_init, rope, ctx):
    shift_m, scale_m, gate_m, shift_f, scale_f, gate_f = jnp.split(mod, 6, axis=-1)
    h = rms_norm(x, p['norm_mix']) * (1.0 + scale_m) + shift_m
    mix, own_ctx = token_mixers(h, p, lam_init, rope, ctx)
    x = x + gate_m * mix
    h = rms_norm(x, p['norm_ffn']) * (1.0 + scale_f) + shift_f
    x = x + gate_f * conv_ffn(h, p)
    return x, own_ctx

def setup_inputs(seed: int = 0) -> dict:
    key = jax.random.key(seed)
    ks = iter(jax.random.split(key, 40))

    def nrm(shape, scale=1.0):
        return jax.random.normal(next(ks), shape, jnp.float32) * scale

    def gain(shape):
        return 1.0 + nrm(shape, 0.05)

    L, D = DEPTH, D_MODEL
    return {
        'x_prompt': nrm((BATCH, SEQ, D)),
        'x_sample': nrm((DEC_BATCH, DEC_SEQ, D)),
        'c': nrm((DEC_BATCH, D)),
        'cache_diff_k': nrm((DEC_BATCH, L, PAST_LEN, 2, DIFF_HEADS, HEAD_DIM)),
        'cache_diff_v': nrm((DEC_BATCH, L, PAST_LEN, DIFF_HEADS, DIFF_V_DIM)),
        'cache_mla_ckv': nrm((DEC_BATCH, L, PAST_LEN, MLA_KV_RANK)),
        'cache_mla_kpe': nrm((DEC_BATCH, L, PAST_LEN, MLA_ROPE_DIM)),
        'cache_gqa_k': nrm((DEC_BATCH, L, PAST_LEN, GQA_KV_HEADS, HEAD_DIM)),
        'cache_gqa_v': nrm((DEC_BATCH, L, PAST_LEN, GQA_KV_HEADS, HEAD_DIM)),
        'c_ctx': nrm((D,)),
        'w_ada': nrm((L, D, 6 * D), 0.5 * D ** -0.5),
        'b_ada': nrm((L, 6 * D), 0.02),
        'norm_mix': gain((L, D)),
        'w_in': nrm((L, D, IN_COLS), D ** -0.5),
        'diff_qk_norm': gain((L, 2, HEAD_DIM)),
        'diff_lambda': nrm((L, 4, HEAD_DIM), 0.1),
        'diff_out_norm': gain((L, DIFF_V_DIM)),
        'mla_q_norm': gain((L, MLA_Q_RANK)),
        'w_mla_q_up': nrm((L, MLA_Q_RANK, MLA_HEADS * MLA_QK_DIM), MLA_Q_RANK ** -0.5),
        'mla_kv_norm': gain((L, MLA_KV_RANK)),
        'w_mla_kv_up': nrm((L, MLA_KV_RANK, MLA_HEADS * (MLA_NOPE_DIM + MLA_V_DIM)), MLA_KV_RANK ** -0.5),
        'mla_qk_norm': gain((L, 2, MLA_QK_DIM)),
        'gqa_qk_norm': gain((L, 2, HEAD_DIM)),
        'w_branch_a': nrm((L, A_WIDTH, D), A_WIDTH ** -0.5),
        'w_branch_b': nrm((L, B_WIDTH, D), B_WIDTH ** -0.5),
        'w_branch_c': nrm((L, C_WIDTH, D), C_WIDTH ** -0.5),
        'w_o': nrm((L, D, D), D ** -0.5),
        'norm_ffn': gain((L, D)),
        'w_up': nrm((L, D, 2 * D_FF), D ** -0.5),
        'conv_w': nrm((L, CONV_WIDTH, 2 * D_FF), CONV_WIDTH ** -0.5),
        'conv_b': nrm((L, 2 * D_FF), 0.02),
        'w_down': nrm((L, D_FF, D), D_FF ** -0.5),
    }

def reference(x_prompt, x_sample, c, cache_diff_k, cache_diff_v, cache_mla_ckv, cache_mla_kpe,
              cache_gqa_k, cache_gqa_v, c_ctx, w_ada, b_ada, norm_mix, w_in, diff_qk_norm,
              diff_lambda, diff_out_norm, mla_q_norm, w_mla_q_up, mla_kv_norm, w_mla_kv_up,
              mla_qk_norm, gqa_qk_norm, w_branch_a, w_branch_b, w_branch_c, w_o, norm_ffn,
              w_up, conv_w, conv_b, w_down):
    t_lat = x_sample.shape[1]
    rope = (axial_rope_tables(t_lat, HEAD_DIM), axial_rope_tables(t_lat, MLA_ROPE_DIM))
    y_p, y_s = x_prompt, x_sample
    states = []
    for l in range(DEPTH):
        p = {
            'norm_mix': norm_mix[l], 'w_in': w_in[l], 'diff_qk_norm': diff_qk_norm[l],
            'diff_lambda': diff_lambda[l], 'diff_out_norm': diff_out_norm[l],
            'mla_q_norm': mla_q_norm[l], 'w_mla_q_up': w_mla_q_up[l],
            'mla_kv_norm': mla_kv_norm[l], 'w_mla_kv_up': w_mla_kv_up[l],
            'mla_qk_norm': mla_qk_norm[l], 'gqa_qk_norm': gqa_qk_norm[l],
            'w_branch_a': w_branch_a[l], 'w_branch_b': w_branch_b[l], 'w_branch_c': w_branch_c[l],
            'w_o': w_o[l], 'norm_ffn': norm_ffn[l], 'w_up': w_up[l], 'conv_w': conv_w[l],
            'conv_b': conv_b[l], 'w_down': w_down[l],
        }
        lam_init = 0.8 - 0.6 * math.exp(-0.3 * l)
        mod_ctx = (jax.nn.silu(c_ctx) @ w_ada[l] + b_ada[l])[None, None, :]
        mod_lat = (jax.nn.silu(c) @ w_ada[l] + b_ada[l])[:, None, :]
        y_p, own_ctx = trunk_layer(y_p, mod_ctx, p, lam_init, None, None)
        states.append(own_ctx)
        ctx = (cache_diff_k[:, l], cache_diff_v[:, l], cache_mla_ckv[:, l], cache_mla_kpe[:, l],
               cache_gqa_k[:, l], cache_gqa_v[:, l])
        y_s, _ = trunk_layer(y_s, mod_lat, p, lam_init, rope, ctx)
    new_diff_k = jnp.stack([s[0] for s in states], axis=1)
    new_diff_v = jnp.stack([s[1] for s in states], axis=1)
    new_mla_ckv = jnp.stack([s[2] for s in states], axis=1)
    new_mla_kpe = jnp.stack([s[3] for s in states], axis=1)
    new_gqa_k = jnp.stack([s[4] for s in states], axis=1)
    new_gqa_v = jnp.stack([s[5] for s in states], axis=1)
    return (y_p, y_s, new_diff_k, new_diff_v, new_mla_ckv, new_mla_kpe, new_gqa_k, new_gqa_v)


_drawn_inputs = setup_inputs


def setup_inputs(seed=0):
    import zlib

    import numpy as np

    out = dict(_drawn_inputs(seed))
    spreads = {}
    factors = {'cache_mla_ckv': 7.926,
     'cache_mla_kpe': 8.0,
     'cache_gqa_k': 8.0,
     'cache_gqa_v': 7.77,
     'diff_lambda': 8.0,
     'diff_out_norm': 6.109,
     'mla_q_norm': 8.0,
     'mla_kv_norm': 8.0,
     'mla_qk_norm': 8.0,
     'norm_ffn': 2.693,
     'conv_b': 7.05}
    for name, (base, spread) in spreads.items():
        noise = np.random.default_rng([zlib.crc32(name.encode()), seed]).standard_normal(out[name].shape)
        drawn = base * np.exp(spread * noise) if base else spread * noise
        out[name] = __import__('jax').numpy.asarray(drawn.astype(out[name].dtype))
    for name, factor in factors.items():
        out[name] = (out[name] * factor).astype(out[name].dtype)
    return out
```

```python
import math
from contextlib import ExitStack

import numpy as np

import concourse.bass as bass
from concourse import mybir

F32 = mybir.dt.float32
F32R = mybir.dt.float32r
ALU = mybir.AluOpType
ACT = mybir.ActivationFunctionType
AX = mybir.AxisListType
ds = bass.ds

P = 128
D, DEPTH, SEQ, DEC, PAST = 1024, 2, 128, 512, 128
HD, NH, VD = 64, 4, 128
QR, KVR, NOPE, ROPE, MH = 256, 128, 64, 32, 8
QK = NOPE + ROPE
GH, GKV = 8, 2
FF = 2816
EPS = 1e-6
GRID_W, BASE = 64, 10000.0
T = SEQ + DEC
NT = T // P
KEYS = SEQ + PAST + DEC
NK = KEYS // P
KD = D // P
HALF = T // 2
OFF = 512 - HALF
FT = FF // P
FPARTS = [(0, 12), (12, 10)]
SUB = 1024
AQ, AK, AV, BQ, BKV, CQ, CK, GATE = 0, 512, 1024, 1536, 1792, 1952, 2464, 2720
BW = QR + KVR + ROPE
P_ADA, P_NM, P_NF, P_CB, P_DN, P_W = 0, 48, 56, 64, 108, 109
NPAR = 109 + 3 * 44
G_DQ, G_DK, G_GQ, G_GK, G_MQ, G_MK, G_BQ, G_BKV, G_LC = 0, 64, 128, 192, 256, 352, 448, 704, 832
NGAIN = 834
GATE_SLOTS = 6


def build_plan():
    plan = []
    pending = []
    count = dict(unit=0, split=0, gemm=0, item=0, score=0, gate=0)

    def add(kind, **k):
        plan.append(dict(step=kind, **k))

    def queue(src, widths, **k):
        for j, w in enumerate(widths):
            pending.append((src if j == 0 else None, w, sum(widths[:j]), j == len(widths) - 1, k))

    def prefetch(ahead):
        while pending and count["split"] < count["gemm"] + ahead:
            src, w, off, last, k = pending.pop(0)
            cols = k.get("cols")
            if src:
                add("unit", src=src, slot=count["unit"] % 2, a=0, **k)
                count["unit"] += 1
            add("split", slot=(count["unit"] - 1) % 2, sub=count["split"] % 2, off=off, width=w, last=last, cols=cols)
            count["split"] += 1

    def gemm(kind, **k):
        prefetch(2)
        add(kind, sub=count["gemm"] % 2, **k)
        count["gemm"] += 1

    def queue_tm(col, w):
        for u in range(2):
            queue("tm", [2 * w] * 2, col=col, w=w, u=u)

    def queue_gates(b, first, n):
        for u in range(n):
            queue("gate", [SUB] * 2, col=GATE + b * D + (first + 2 * u) * P, cols=(KD, P))

    def gate():
        gemm("gate", g=count["gate"] % KD)
        count["gate"] += 1

    def item(kind, width, groups, gains, rope, tile, **k):
        it = dict(kind=kind, width=width, groups=groups, gains=gains, rope=rope, tile=tile, bank=tile, **k)
        if groups:
            it["slot"], it["par"] = count["item"] % 5, count["item"] % 2
            count["item"] += 1
        return it

    def chunk(w, first, prev):
        for i, it in enumerate(prev):
            add("acc", it=it)
            if i == 1:
                prefetch(2)
        for s in range(4):
            gemm("tm", w=w, s=s, first=first)
            for it in prev[2 * s:2 * s + 2]:
                add("tick", it=it)
            if s == 2 and prev:
                add("flush")
            if s >= 1:
                for it in prev[2 * (s - 1):2 * s]:
                    add("turn", it=it)

    def finish(its):
        for it in its:
            add("acc", it=it)
        for it in its[0:2]:
            add("tick", it=it)
        gate()
        for it in its[2:4]:
            add("tick", it=it)
        for it in its[0:2]:
            add("turn", it=it)
        add("tick", it=its[4])
        add("flush")
        gate()
        for it in its[2:]:
            add("turn", it=it)

    def attention(br, heads, fill):
        seq = [(h, q) for h in heads for q in range(NT)]
        ns, lag = (2, 1) if br == "A" else (1, 2)
        start = count["score"]
        count["score"] += ns * len(seq)
        for i in range(len(seq) + lag):
            if i < len(seq):
                for m in range(ns):
                    add("score", br=br, h=seq[i][0], q=seq[i][1], m=m, n=start + i * ns + m, first=i == m == 0)
            if 1 <= i <= len(seq):
                add("soft", br=br, q=seq[i - 1][1], n=start + (i - 1) * ns, back=ns if i < len(seq) else 0)
            if i >= lag:
                h, q = seq[i - lag]
                add("turnp", br=br, q=q, n=start + (i - lag) * ns, first=i == lag)
                if q == NT - 1:
                    for _ in range(fill.get(h, 0)):
                        gate()
                    add("values", br=br, h=h)

    def branch(b):
        add("osplit")
        for k in range(KD // 2):
            if k == 2:
                gate()
                gate()
            gemm("branch", b=b, k=k)
            add("merge", b=b, k=k)

    def queue_branch(b):
        queue("branch", [SUB] * 2, b=b, u=0, cols=(4, 2 * P))
        queue_gates(b, 6, 1)
        queue("branch", [SUB] * 2, b=b, u=1, cols=(4, 2 * P))

    add("params")
    add("loop", n=12, body=[x for s in (0, 1) for x in
                            (dict(step="unit", src="ada", slot=s, a=s), dict(step="ada", slot=s, a=s))])
    add("mod")
    for c in (AQ, AK, AV):
        queue_tm(c, 512)
    queue_gates(0, 0, 3)
    queue_branch(0)
    prefetch(1)
    add("norm", which=0)

    aq = [item("aq", 512, [(0, 8, HD)], [G_DQ], "h" if t else None, t) for t in range(NT)]
    ak = [item("ak", 512, [(0, 8, HD)], [G_DK], "h" if t else None, t) for t in range(NT)]
    add("cache", b=0)
    chunk(512, True, [])
    chunk(512, False, aq)
    add("turnc", b=0)
    chunk(512, False, ak)
    for t in range(NT):
        add("acc", it=item("av", 512, [], [], None, t))
    attention("A", range(NH), {h: 1 for h in range(NH)})
    for h in range(NH):
        add("ostat", h=h)
        if h % 2 == 0:
            gate()
        add("obcast", h=h)
    queue_tm(BQ, BW)
    queue_gates(1, 0, 1)
    branch(0)

    cached = item("bc", BW, [(QR, 1, KVR)], [G_BKV], None, 1)
    bq = [item("bq", BW, [(0, 1, QR), (QR, 1, KVR)], [G_BQ, G_BKV], None, t) for t in range(NT)]
    add("cache", b=1)
    add("acc", it=cached)
    add("tick", it=cached)
    add("flush")
    for s in range(4):
        gemm("tm", w=BW, s=s, first=True)
        if s == 0:
            add("turn", it=cached)
    finish(bq)
    for half in range(2):
        slot = count["unit"] % 2
        add("unit", src="mla", slot=slot, half=half, a=0)
        count["unit"] += 1
        queue_gates(1, 2 + 2 * half, 1)
        prefetch(1)
        its = [item("up", 4 * QK, [(0, 4, QK)], [G_MQ], "r" if t else None, t, q=True) for t in range(NT)]
        its += [item("up", 4 * QK, [(0, 4, QK)], [G_MK], "r" if t > 1 else None, t, q=False) for t in range(NK)]
        for i, it in enumerate(its):
            it["last"] = i == len(its) - 1
            it["slot_raw"] = slot
            it["bank"] = i % 4
            add("upmm", it=it, i=i, half=half)
            add("acc", it=it)
            add("tick", it=it)
            if i in (4, 9):
                gate()
            if i >= 2:
                add("turn", it=its[i - 2])
        add("flush")
        add("turn", it=its[-2])
        add("turn", it=its[-1])
        if half:
            queue_branch(1)
            for c, w in ((CK, 256), (CQ, 512)):
                queue_tm(c, w)
            queue_gates(2, 0, 3)
            queue_branch(2)
        attention("B", range(4 * half, 4 * half + 4), {})
    branch(1)

    ck = [item("ck", 256, [(0, 2, HD)], [G_GK], "h" if t else None, t) for t in range(NT)]
    cq = [item("cq", 512, [(0, 8, HD)], [G_GQ], "h" if t else None, t) for t in range(NT)]
    add("cache", b=2)
    add("turnc", b=2)
    chunk(256, True, [])
    chunk(512, False, ck)
    finish(cq)
    attention("C", range(GH), {1: 1, 3: 1, 5: 1, 6: 1})
    branch(2)
    add("msplit")

    def fm_units(kind, n, width, **k):
        assert not pending and count["unit"] % 2 == 0 and count["gemm"] == count["split"]

        def unit(s, a, first=False):
            out = [dict(step="unit", src=kind, slot=s, a=a, **k)]
            for j in range(2):
                out.append(dict(step="split", slot=s, sub=j, off=j * width, width=width, last=j == 1,
                                cols=(KD, P) if kind == "wo" else None))
                out.append(dict(step=kind, sub=j, s=s, a=a, first=first, **k))
            return out

        def over(s, a, unit_before):
            u = unit(s, a)
            out = [dict(step=kind + "_out", s=1 - s, a=unit_before, **k)]
            out2 = [dict(step=kind + "_out2", s=1 - s, a=unit_before, **k)]
            return u[:2] + out + u[2:4] + out2 + u[4:]

        plan.extend(unit(0, 0, first=True))
        add("loop", n=n // 2 - 1, body=over(1, 1, 0) + over(0, 2, 1))
        plan.extend(over(1, n - 1, n - 2))
        plan.append(dict(step=kind + "_out", s=1, a=n - 1, **k))
        plan.append(dict(step=kind + "_out2", s=1, a=n - 1, **k))
        count["unit"] += n

    fm_units("wo", KD // 2, SUB)
    add("norm", which=1)
    for f0, nf in FPARTS:
        fm_units("up", nf, SUB, f0=f0, nf=nf)
        fm_units("down", KD, nf // 2 * P, f0=f0, nf=nf)
    assert count["unit"] % 2 == 0 and count["gate"] == 3 * KD
    look_back(plan)
    return plan


def look_back(plan):
    splits, los, gemms, accs, ticks, softs, raws = 0, 0, 0, [], [], [], {0: 0, 1: 0}
    made = []
    for s in plan:
        k = s["step"]
        if k == "loop":
            look_back(s["body"])
        elif k == "split":
            s["ahead"] = splits - gemms
            splits += 1
            if s["last"]:
                raws[s["slot"]] += 1
            else:
                los += 1
            made.append(dict(number=splits, last=s["last"], slot=s["slot"], raw=raws[s["slot"]], lo=los))
        elif k in ("tm", "gate", "branch", "wo", "up", "down"):
            m = made.pop(0)
            s["hi_back"] = splits - m["number"]
            s["lo_name"] = f"raw_done{m['slot']}" if m["last"] else "lo_ready"
            s["lo_back"] = raws[m["slot"]] - m["raw"] if m["last"] else los - m["lo"]
            gemms += 1
        elif k == "ada":
            raws[s["slot"]] += 1
        elif k == "upmm" and s["it"]["last"]:
            raws[s["it"]["slot_raw"]] += 1
        elif k == "acc":
            accs.append(id(s["it"]))
        elif k == "tick":
            s["acc_back"] = len(accs) - 1 - accs.index(id(s["it"]))
            ticks.append(id(s["it"]))
        elif k == "turn":
            s["item_back"] = len(ticks) - 1 - ticks.index(id(s["it"]))
        elif k == "soft":
            softs.append(s["n"])
        elif k == "turnp":
            s["p_back"] = len(softs) - 1 - softs.index(s["n"])


def signals(s):
    k = s["step"]
    it = s.get("it")
    if k == "params":
        return dict(rows_loaded=16 * 7, gains_loaded=16 * 7, rows_turned=1, par_ready=1, gain_ready=3, lam_step=5, lam_exp=1)
    if k == "unit":
        return {f"raw_full{s['slot']}": 32 if s["src"] in ("mla", "up") else 16}
    if k == "ada":
        return {f"raw_done{s['slot']}": 1}
    if k == "mod":
        return dict(mod_ready=3)
    if k == "norm":
        return dict(sq_ready=KD, stat_done=KD, nms_ready=1, nrs_ready=1, diag_ready=NT, bc_done=1, xn_done=KD,
                    hf_ready=KD, hhi_ready=KD, hlo_ready=KD)
    if k == "split":
        return {"hi_ready": 1, (f"raw_done{s['slot']}" if s["last"] else "lo_ready"): 1}
    if k == "tm":
        return dict(sub_done=1, acc_done=NT - 1 if s["s"] == 3 else 0)
    if k in ("gate", "branch", "wo", "up", "down"):
        return dict(sub_done=1, **(dict(gate_ready=1) if k == "gate" else {}))
    if k == "cache":
        return dict(cache_loaded=32)
    if k == "turnc":
        return dict(t_done=1, t_copied=1)
    if k == "acc":
        out = dict(acc_copied=1)
        if it["tile"] == 0:
            out["ctx_out"] = {"av": 16, "ck": 16, "bq": 32}.get(it["kind"], 0)
        return out
    if k == "tick":
        out = dict(sqr_done=1, ss_ready=len(it["groups"]), ms_done=len(it["groups"]), rstd_ready=1, xh_ready=1)
        if it["rope"]:
            out.update(gained=1, sin_ready=1, cos_done=1)
        return dict(out, item_ready=1)
    if k == "turn":
        out = dict(t_done=1, t_copied=1)
        if it["tile"] == 0:
            out["ctx_out"] = {"ak": 16, "ck": 16}.get(it["kind"], 0)
        return out
    if k == "upmm":
        return {f"raw_done{it['slot_raw']}" if it["last"] else "up_done": 1}
    if k == "score":
        return dict(score_done=1, max_ready=1, exp_done=1)
    if k == "soft":
        return dict(rden_done=1, p_ready=1, p1_done=1 if s["br"] == "A" else 0)
    if k == "turnp":
        return dict(pt_done=1, pt_copied=1)
    if k == "values":
        return dict(av_done=1, ot_copied=1)
    if k == "ostat":
        return dict(osq_ready=1, ostat_done=1, oms_ready=1, ors_ready=1, odiag_ready=NT)
    if k == "obcast":
        return dict(obc_done=1, on_ready=1)
    if k == "osplit":
        return dict(ohi_ready=4, olo_ready=4)
    if k == "merge":
        return dict(fm_read=2, mg_ready=2 if s["b"] else 0)
    if k == "msplit":
        return dict(mhi_ready=KD, mlo_ready=KD)
    if k in ("wo_out",):
        return dict(fm_read=2)
    if k == "down_out":
        return dict(fm_read=1)
    if k == "up_out":
        return dict(v_ready=2, tap_done=2, fm_read=2)
    if k == "up_out2":
        return dict(silu_done=1, prod_ready=1, ahi_ready=1, alo_ready=1)
    return {}


def total(plan):
    out = {}
    for s in plan:
        for name, n in (total(s["body"]) if s["step"] == "loop" else signals(s)).items():
            out[name] = out.get(name, 0) + n * (s["n"] if s["step"] == "loop" else 1)
    return out


CREDIT = 2
PLAN = build_plan()
PER_LAYER = total(PLAN)


class Count:

    def __init__(self, layer):
        self.layer, self.n, self.turn, self.per_turn = layer, {}, 0, {}

    def __call__(self, name, more=0):
        v = self.n.get(name, 0) + more + (0 if name in DMA_SEMS else CREDIT)
        v = self.layer * PER_LAYER[name] + v
        if self.per_turn.get(name, 0):
            v = v + self.turn * self.per_turn[name]
        return v

    def past(self, s, times=1):
        for name, n in (total(s["body"]) if s["step"] == "loop" else signals(s)).items():
            self.n[name] = self.n.get(name, 0) + n * times


DMA_SEMS = {"rows_loaded", "gains_loaded", "raw_full0", "raw_full1", "cache_loaded", "ctx_out"}


def walk(eng, plan, wanted, emit, count):
    for s in plan:
        if s["step"] == "loop":
            if any(x["step"] in wanted for x in s["body"]):
                with eng.Fori(0, s["n"]) as turn:
                    count.turn, count.per_turn = turn, total(s["body"])
                    before = dict(count.n)
                    for x in s["body"]:
                        if x["step"] in wanted:
                            emit(x)
                        count.past(x)
                    count.n, count.turn, count.per_turn = before, 0, {}
            count.past(s, s["n"])
        else:
            if s["step"] in wanted:
                emit(s)
            count.past(s)


def turn_parts(it):
    return {"aq": [(i * P, P) for i in range(4)], "ak": [(i * P, P) for i in range(4)],
            "cq": [(i * P, P) for i in range(4)], "ck": [(0, P)], "bq": [(0, P), (P, P), (QR, P)], "bc": [(QR, P)],
            "up": [(i * QK, QK) for i in range(4)]}[it["kind"]]


def key_tile(it):
    return it["tile"] if it["kind"] in ("up", "bc") or not it["tile"] else it["tile"] + 1


def latent_tile(it):
    return it["tile"] - (2 if it["kind"] == "up" and not it["q"] else 1)


def span(it):
    a = it["groups"][0][0]
    b = it["groups"][-1]
    return a, b[0] + b[1] * b[2]


def program(nc, x_ctx, x_lat, c_lat, cache_dk, cache_dv, cache_ckv, cache_kpe, cache_gk, cache_gv, c_ctx,
            w_ada, b_ada, norm_mix, w_in, diff_qk_norm, diff_lambda, diff_out_norm, mla_q_norm, w_mla_q_up,
            mla_kv_norm, w_mla_kv_up, mla_qk_norm, gqa_qk_norm, w_a, w_b, w_c, w_o, norm_ffn, w_up, conv_w,
            conv_b, w_down, const_ident, const_rope_h, const_rope_r, const_layer,
            y_ctx, y_lat, new_dk, new_dv, new_ckv, new_kpe, new_gk, new_gv):
    ctx = ExitStack()
    with ctx:
        def sb(name, shape, dt=F32):
            return ctx.enter_context(nc.sbuf_tensor(name, shape, dt))

        def over(*groups):
            out, most = [], 0
            for g in groups:
                with ExitStack() as st:
                    size = 0
                    for name, shape, dt in g:
                        out.append(st.enter_context(nc.sbuf_tensor(name, shape, dt)))
                        size += int(np.prod(shape[1:])) * 4
                    most = max(most, size)
            sb("room_" + groups[0][0][0], [P, most // 4])
            return out

        ident, ones = sb("ident", [P, P]), sb("ones", [P, P])
        xT = sb("xT", [P, KD, T])
        hhi, hlo = sb("hhi", [P, KD, T], F32R), sb("hlo", [P, KD, T], F32R)
        raw = sb("raw", [P, 2, 2 * SUB])
        whi, wlo = sb("whi", [P, 2, SUB], F32R), sb("wlo", [P, 2, SUB], F32R)
        rows = sb("rows", [P, 3, P])
        PT = sb("PT", [P, NPAR])
        gains = sb("gains", [P, NGAIN])
        lamv = sb("lamv", [P, 4, HD])
        lam2, lame, neglam, dgain = sb("lam2", [P, 2]), sb("lame", [P, 2]), sb("neglam", [P, 1]), sb("dgain", [P, 1])
        mod = sb("mod", [P, 6 * KD, 2])
        scale = sb("scale", [P, 2, KD, 2])
        cT = sb("cT", [P, KD, 2])
        crow = sb("crow", [2 * KD, P])
        ropeh, roper = sb("ropeh", [P, NT - 1, 2, HD]), sb("roper", [P, NT - 1, 2, ROPE])
        ckv_out = sb("ckv_out", [P, KVR + ROPE])
        epsc, mhalf = sb("epsc", [P, 1]), sb("mhalf", [P, 8])
        ssum, smean, rstd = sb("ssum", [P, 2, 8]), sb("smean", [P, 2, 8]), sb("rstd", [P, 2, 8])
        negmax, den, rden = sb("negmax", [P, 4]), sb("den", [P, 4]), sb("rden", [P, 4])
        nmean, nrstd = sb("nmean", [P, NT]), sb("nrstd", [P, NT])

        (stage, tmpq, tmpc, tmps, prob, probT, probTc, ohi, olo, nsq, hf, diag) = over(
            [("stage", [P, 5, 512], F32), ("tmpq", [P, 512], F32), ("tmpc", [P, 512], F32), ("tmps", [P, 512], F32)],
            [("prob", [P, 4, T], F32), ("probT", [P, NT, DEC], F32), ("probTc", [P, P], F32)],
            [("ohi", [P, 4, T], F32R), ("olo", [P, 4, T], F32R)],
            [("nsq", [P, 2, T], F32), ("hf", [P, 2, T], F32), ("diag", [P, NT, P], F32)])
        mixers = [("merged", [P, KD, T], F32), ("gated", [P, GATE_SLOTS, T], F32), ("oT", [P, 4, T], F32)]
        branches = [[("qA", [P, 4, T], F32), ("kA", [P, 4, KEYS], F32), ("vA", [P, NK, 512], F32)],
                    [("bqT", [P, 2, T], F32), ("ckvT", [P, KEYS], F32), ("kpe", [P, NK, ROPE], F32),
                     ("qB", [P, 4, T], F32), ("kB", [P, 4, KEYS], F32), ("vB", [P, NK, 4, 64], F32)],
                    [("qC", [P, 4, T], F32), ("kC", [P, KEYS], F32), ("vC", [P, NK, 128], F32)]]
        ffn = [("ahi", [P, 12, T], F32R), ("alo", [P, 12, T], F32R), ("va", [P, 2, T], F32), ("vg", [P, 2, T], F32)]
        with ExitStack() as st:
            merged, gated, oT = [st.enter_context(nc.sbuf_tensor(*x)) for x in mixers]
            made = []
            for g in branches:
                with ExitStack() as st2:
                    made += [st2.enter_context(nc.sbuf_tensor(*x)) for x in g]
        (qA, kA, vA, bqT, ckvT, kpe, qB, kB, vB, qC, kC, vC) = made
        size = max(sum(int(np.prod(x[1][1:])) for x in mixers + g) for g in branches)
        (ahi, alo, va, vg, xin, room) = over(ffn, [("xin", [P, NT, D], F32)], [("mixroom", [P, size], F32)])
        cached = oT[:, :, :].rearrange("p a b -> p (a b)")
        ps = ctx.enter_context(nc.psum_tensor("ps", [P, 8 * 512], F32))

        def bank(b, n=512, p0=0, p1=P):
            return ps[p0:p1, b * 512:b * 512 + n]

        def run(pair, lo=0, hi=T, p0=0, p1=P):
            return ps[p0:p1, pair * 1024 + OFF + lo:pair * 1024 + OFF + hi]

        def halves(pair):
            return [(run(pair, 0, HALF), 0), (run(pair, HALF, T), HALF)]

        def line(pair, n=T, p0=0, p1=P, off=0):
            return ps[p0:p1, pair * 1024 + off:pair * 1024 + off + n]

        def sub_views(s):
            slot, w, sub = s["slot"], s["width"], s["sub"]
            if s["cols"]:
                k, c = s["cols"]
                j = 1 if s["last"] else 0
                src = raw[:, slot, :].rearrange("p (k c) -> p k c", k=k)[:, :, j * c:(j + 1) * c]
                return src, lambda x: x[:, sub, :].rearrange("p (k c) -> p k c", k=k)
            return raw[:, slot, s["off"]:s["off"] + w], lambda x: x[:, sub, 0:w]

        def rope_views(it):
            c, nh, dh = it["groups"][0]
            r0, half = (0, HD // 2) if it["rope"] == "h" else (NOPE, ROPE // 2)
            table = ropeh if it["rope"] == "h" else roper
            w = 2 * half
            x = stage[:, it["slot"], 0:nh * dh].rearrange("p (h d) -> p h d", h=nh)[:, :, r0:r0 + w]
            cs = [table[:, latent_tile(it), j, :].unsqueeze(1).to_broadcast([P, nh, w]) for j in range(2)]
            tc, ts = [x_[:, 0:nh * w].rearrange("p (h d) -> p h d", h=nh) for x_ in (tmpc, tmps)]
            return r0, half, x, cs, tc, ts

        sems = {n: ctx.enter_context(nc.semaphore(n)) for n in list(PER_LAYER) +
                ["const_loaded", "const_set", "x_loaded", "x_turned", "x_copied", "c_turned", "c_ready",
                 "y_turned", "y_copied", "y_out"]}
        S = sems
        block = ctx.enter_context(nc.Block())

        @block.sync
        def _(sp):
            sp.dma_start(ident[:, :], const_ident).then_inc(S["const_loaded"], 16)
            sp.dma_start(crow[0:KD, :], c_ctx.rearrange("(k p) -> k p", p=P)).then_inc(S["const_loaded"], 16)
            sp.dma_start(crow[KD:2 * KD, :], c_lat.rearrange("a (k p) -> (a k) p", p=P)).then_inc(S["const_loaded"], 16)
            sp.dma_start(xin[:, 0, :], x_ctx[0]).then_inc(S["x_loaded"], 16)
            sp.dma_start(xin[:, 1:NT, :], x_lat[0].rearrange("(t p) d -> p t d", p=P)).then_inc(S["x_loaded"], 16)
            sp.dma_start(ropeh[:, :, :, :], const_rope_h).then_inc(S["const_loaded"], 16)
            sp.dma_start(roper[:, :, :, :], const_rope_r).then_inc(S["const_loaded"], 16)
            with sp.Fori(0, DEPTH) as layer:
                n = Count(layer)

                def at(x):
                    return x[ds(layer, 1)]

                def row(x, a, b):
                    return at(x)[:, a:b]

                def load_params():
                    sp.wait_ge(S["par_ready"], n("par_ready"))
                    sp.wait_ge(S["hlo_ready"], n("hlo_ready"))
                    for at_row, x, k in ((P_ADA, b_ada, 48), (P_NM, norm_mix, KD), (P_NF, norm_ffn, KD), (P_CB, conv_b, 44),
                                         (P_DN, diff_out_norm, 1)):
                        sp.dma_start(rows[at_row:at_row + k, 0, :], at(x).rearrange("l (k p) -> (l k) p", p=P))\
                          .then_inc(S["rows_loaded"], 16)
                    sp.dma_start(rows[0:88, 1, :], at(conv_w)[:, 0:2, :].rearrange("l w (k p) -> (l w k) p", p=P))\
                      .then_inc(S["rows_loaded"], 16)
                    sp.dma_start(rows[0:44, 2, :], at(conv_w)[:, 2:3, :].rearrange("l w (k p) -> (l w k) p", p=P))\
                      .then_inc(S["rows_loaded"], 16)
                    for g, x, k in ((G_DQ, at(diff_qk_norm).rearrange("l a b -> l (a b)"), 2 * HD),
                                    (G_GQ, at(gqa_qk_norm).rearrange("l a b -> l (a b)"), 2 * HD),
                                    (G_MQ, at(mla_qk_norm).rearrange("l a b -> l (a b)"), 2 * QK),
                                    (G_BQ, at(mla_q_norm), QR), (G_BKV, at(mla_kv_norm), KVR),
                                    (G_LC, at(const_layer), 2)):
                        sp.dma_start(gains[:, g:g + k], x.to_broadcast([P, k])).then_inc(S["gains_loaded"], 16)
                    sp.dma_start(lamv[:, :, :].rearrange("p a b -> p (a b)"),
                                 at(diff_lambda).rearrange("l a b -> l (a b)").to_broadcast([P, 4 * HD]))\
                      .then_inc(S["gains_loaded"], 16)

                def load_unit(s):
                    src, slot = s["src"], s["slot"]
                    full = S[f"raw_full{slot}"]
                    r = raw[:, slot, :]
                    sp.wait_ge(S[f"raw_done{slot}"], n(f"raw_done{slot}"))
                    u = n.turn * 2 + s["a"]
                    if src == "ada":
                        sp.dma_start(r.rearrange("p (k c) -> p k c", k=KD),
                                     at(w_ada)[:, :, ds(u * 256, 256)].rearrange("l (k p) c -> p (l k) c", p=P)).then_inc(full, 16)
                    elif src == "tm":
                        w = s["w"]
                        sp.dma_start(r[:, 0:4 * w].rearrange("p (k c) -> p k c", k=4),
                                     at(w_in)[:, s["u"] * 512:(s["u"] + 1) * 512, s["col"]:s["col"] + w]
                                     .rearrange("l (k p) c -> p (l k) c", p=P)).then_inc(full, 16)
                    elif src == "gate":
                        sp.dma_start(r.rearrange("p (k c) -> p k c", k=KD), at(w_in)[:, :, s["col"]:s["col"] + 256]
                                     .rearrange("l (k p) c -> p (l k) c", p=P)).then_inc(full, 16)
                    elif src == "branch":
                        w = (w_a, w_b, w_c)[s["b"]]
                        sp.dma_start(r.rearrange("p (k c) -> p k c", k=4),
                                     at(w)[:, :, s["u"] * 512:(s["u"] + 1) * 512]
                                     .rearrange("l (k p) c -> p (l k) c", p=P)).then_inc(full, 16)
                    elif src == "mla":
                        h = s["half"]
                        sp.dma_start(r[:, 0:768].rearrange("p (k c) -> p k c", k=2),
                                     at(w_mla_q_up)[:, :, h * 384:(h + 1) * 384].rearrange("l (k p) c -> p (l k) c", p=P))\
                          .then_inc(full, 16)
                        sp.dma_start(r[:, 768:1280], at(w_mla_kv_up)[:, :, h * 512:(h + 1) * 512]
                                     .rearrange("l p c -> p (l c)")).then_inc(full, 16)
                    elif src == "wo":
                        sp.dma_start(r.rearrange("p (k c) -> p k c", k=KD), at(w_o)[:, :, ds(u * 256, 256)]
                                     .rearrange("l (k p) c -> p (l k) c", p=P)).then_inc(full, 16)
                    elif src == "up":
                        for j in range(2):
                            sp.dma_start(r[:, j * SUB:(j + 1) * SUB].rearrange("p (k c) -> p k c", k=KD),
                                         at(w_up)[:, :, ds((u + s["f0"]) * P + j * FF, P)]
                                         .rearrange("l (k p) c -> p (l k) c", p=P)).then_inc(full, 16)
                    elif src == "down":
                        nf, f0 = s["nf"], s["f0"]
                        sp.dma_start(r[:, 0:nf * P].rearrange("p (k c) -> p k c", k=nf),
                                     at(w_down)[:, f0 * P:(f0 + nf) * P, ds(u * P, P)]
                                     .rearrange("l (k p) c -> p (l k) c", p=P)).then_inc(full, 16)

                def emit(s):
                    if s["step"] == "params":
                        load_params()
                    else:
                        load_unit(s)

                walk(sp, PLAN, ("params", "unit"), emit, n)
            for t in range(NT):
                sp.wait_ge(S["y_copied"], 2 * t + 2)
                sp.dma_start(y_ctx[0] if t == 0 else y_lat[0, (t - 1) * P:t * P, :], xin[:, t, :]).then_inc(S["y_out"], 16)
            sp.wait_ge(S["y_out"], 16 * NT)
            sp.wait_ge(S["ctx_out"], DEPTH * PER_LAYER["ctx_out"])

        @block.tensor
        def _(pe):
            pe.wait_ge(S["const_loaded"], 16 * 5)
            pe.wait_ge(S["const_set"], 4)
            pe.transpose(bank(7, 2 * KD), crow[:, :], ident[0:2 * KD, 0:2 * KD]).then_inc(S["c_turned"], 1)
            pe.wait_ge(S["x_loaded"], 32)
            for t in range(NT):
                for j in range(2):
                    if t * 2 + j >= 4:
                        pe.wait_ge(S["x_copied"], t * 2 + j - 3)
                    for i in range(4):
                        f = j * 4 + i
                        mm = pe.transpose(bank((t * 2 + j) % 4)[:, i * P:(i + 1) * P], xin[:, t, f * P:(f + 1) * P], ident[:, :])
                    mm.then_inc(S["x_turned"], 1)
            with pe.Fori(0, DEPTH) as layer:
                n = Count(layer)

                def params(s):
                    pe.wait_ge(S["rows_loaded"], n("rows_loaded", 112))
                    pe.wait_ge(S["fm_read"], n("fm_read"))
                    pe.transpose(line(3, 109), rows[0:109, 0, :], ident[0:109, 0:109])
                    pe.transpose(line(3, 88, off=109), rows[0:88, 1, :], ident[0:88, 0:88])
                    pe.transpose(line(3, 44, off=197), rows[0:44, 2, :], ident[0:44, 0:44]).then_inc(S["rows_turned"], 1)

                def ada(s):
                    slot = s["slot"]
                    pe.wait_ge(S[f"raw_full{slot}"], n(f"raw_full{slot}"))
                    pe.wait_ge(S["c_ready"], 1)
                    for j in range(2):
                        for k in range(KD):
                            mm = pe.matmul(bank(7)[:, ds((n.turn * 2 + s["a"]) * 4 + 2 * j, 2)],
                                           raw[:, slot, k * 256 + j * P:k * 256 + (j + 1) * P], cT[:, k, :],
                                           start=k == 0, stop=k == KD - 1)
                    mm.then_inc(S[f"raw_done{slot}"], 1)

                def spread(out_pair, diag_t, ready, signal):
                    pe.wait_ge(S[ready[0]], ready[1])
                    rhs = diag_t.rearrange("p t c -> p (t c)")
                    for out, c in halves(out_pair):
                        mm = pe.matmul(out, ones[:, :], rhs[:, c:c + HALF], start=True, stop=True)
                    mm.then_inc(S[signal], 1)

                def norm(s):
                    pe.wait_ge(S["fm_read"], n("fm_read"))
                    pe.wait_ge(S["par_ready"], n("par_ready"))
                    pe.wait_ge(S["x_copied"], 2 * NT)
                    for k in range(KD):
                        pe.wait_ge(S["sq_ready"], n("sq_ready", k + 1))
                        for t in range(NT):
                            mm = pe.matmul(bank(6)[:, t:t + 1], nsq[:, k % 2, t * P:(t + 1) * P], ones[:, 0:1],
                                           start=k == t == 0, stop=k == KD - 1, skip_group_check=True)
                        mm.then_inc(S["stat_done"], 1)
                    spread(0, diag[:, :, :], ("diag_ready", n("diag_ready", NT)), "bc_done")

                def sub_waits(s):
                    pe.wait_ge(S["hi_ready"], n("hi_ready", -s["hi_back"]))
                    pe.wait_ge(S[s["lo_name"]], n(s["lo_name"], -s["lo_back"]))

                def tm(s):
                    sub, w = s["sub"], s["w"]
                    sub_waits(s)
                    pe.wait_ge(S["hlo_ready"], n("hlo_ready"))
                    for t in range(NT):
                        if s["s"] == 0:
                            if s["first"]:
                                pe.wait_ge(S["fm_read"], n("fm_read"))
                            else:
                                pe.wait_ge(S["acc_copied"], n("acc_copied", t + 1 - NT))
                        for k in range(2):
                            kt = 2 * s["s"] + k
                            c = slice(t * P, (t + 1) * P)
                            wh, wl = whi[:, sub, k * w:(k + 1) * w], wlo[:, sub, k * w:(k + 1) * w]
                            out = bank(t, w)
                            pe.matmul(out, hhi[:, kt, c], wh, start=kt == 0, stop=False)
                            pe.matmul(out, hhi[:, kt, c], wl, start=False, stop=False)
                            mm = pe.matmul(out, hlo[:, kt, c], wh, start=False, stop=kt == KD - 1)
                        if s["s"] == 3 and t < NT - 1:
                            mm.then_inc(S["acc_done"], 1)
                    mm.then_inc(S["sub_done"], 1)

                def feature_tile(pair, sub, ks, step, off, mh, ml, first=True, last=True):
                    for i, kt in enumerate(ks):
                        c = slice(i * step + off, i * step + off + P)
                        for w, m, a in ((whi, mh, 0), (whi, ml, 1), (wlo, mh, 2)):
                            for out, o in halves(pair):
                                mm = pe.matmul(out, w[:, sub, c], m[:, kt, o:o + HALF],
                                               start=first and i == 0 and a == 0, stop=last and i == len(ks) - 1 and a == 2)
                    return mm

                def gate(s):
                    sub_waits(s)
                    pe.wait_ge(S["gate_ready"], n("gate_ready"))
                    pe.wait_ge(S["ot_copied"], n("ot_copied"))
                    pe.wait_ge(S["on_ready"], n("on_ready"))
                    pe.wait_ge(S["oms_ready"], n("oms_ready"))
                    feature_tile(3, s["sub"], range(KD), P, 0, hhi, hlo).then_inc(S["sub_done"], 1)

                def branch(s):
                    sub_waits(s)
                    if s["k"] == 0:
                        pe.wait_ge(S["ohi_ready"], n("ohi_ready"))
                        pe.wait_ge(S["olo_ready"], n("olo_ready"))
                        pe.wait_ge(S["exp_done"], n("exp_done"))
                        pe.wait_ge(S["pt_copied"], n("pt_copied"))
                    for j in range(2):
                        i = 2 * s["k"] + j
                        if i >= 3:
                            pe.wait_ge(S["fm_read"], n("fm_read", j - 2))
                        mm = feature_tile(i % 3, s["sub"], range(4), 2 * P, j * P, ohi, olo)
                    mm.then_inc(S["sub_done"], 1)

                def fm_waits(s, lag):
                    pe.wait_ge(S["fm_read"], n("fm_read", 0 if s["first"] else -lag))

                def wo(s):
                    sub_waits(s)
                    if s["first"]:
                        pe.wait_ge(S["mlo_ready"], n("mlo_ready"))
                        pe.wait_ge(S["gate_ready"], n("gate_ready"))
                    fm_waits(s, 2)
                    feature_tile(2 * s["s"] + s["sub"], s["sub"], range(KD), P, 0, hhi, hlo).then_inc(S["sub_done"], 1)

                def up(s):
                    sub_waits(s)
                    if s["first"]:
                        pe.wait_ge(S["hlo_ready"], n("hlo_ready"))
                    fm_waits(s, 2)
                    feature_tile(2 * s["s"] + s["sub"], s["sub"], range(KD), P, 0, hhi, hlo).then_inc(S["sub_done"], 1)

                def down(s):
                    sub_waits(s)
                    if s["first"]:
                        pe.wait_ge(S["alo_ready"], n("alo_ready"))
                    fm_waits(s, 1)
                    half = s["nf"] // 2
                    feature_tile(2 * s["s"], s["sub"], range(s["sub"] * half, (s["sub"] + 1) * half), P, 0, ahi, alo,
                                 first=s["sub"] == 0, last=s["sub"] == 1).then_inc(S["sub_done"], 1)

                def turnc(s):
                    pe.wait_ge(S["cache_loaded"], n("cache_loaded"))
                    pe.wait_ge(S["fm_read"], n("fm_read"))
                    pe.wait_ge(S["t_copied"], n("t_copied"))
                    for i in range(4 if s["b"] == 0 else 1):
                        mm = pe.transpose(bank(5)[:, i * P:(i + 1) * P], cached[:, i * P:(i + 1) * P], ident[:, :])
                    mm.then_inc(S["t_done"], 1)

                def turn(s):
                    it = s["it"]
                    src = stage[:, it["slot"], :]
                    pe.wait_ge(S["item_ready"], n("item_ready", -s["item_back"]))
                    pe.wait_ge(S["t_copied"], n("t_copied"))
                    pe.wait_ge(S["pt_copied"], n("pt_copied"))
                    for i, (c, w) in enumerate(turn_parts(it)):
                        mm = pe.transpose(bank(5)[0:w, i * P:(i + 1) * P], src[:, c:c + w], ident[:, :])
                    mm.then_inc(S["t_done"], 1)

                def upmm(s):
                    it, i = s["it"], s["i"]
                    slot = it["slot_raw"]
                    if i == 0:
                        pe.wait_ge(S[f"raw_full{slot}"], n(f"raw_full{slot}"))
                        pe.wait_ge(S["t_copied"], n("t_copied"))
                        pe.wait_ge(S["exp_done"], n("exp_done"))
                        pe.wait_ge(S["acc_copied"], n("acc_copied"))
                    if i >= 4:
                        pe.wait_ge(S["acc_copied"], n("acc_copied", -3))
                    t = it["tile"]
                    if it["q"]:
                        for k in range(2):
                            mm = pe.matmul(bank(i % 4, 384), bqT[:, k, t * P:(t + 1) * P],
                                           raw[:, slot, k * 384:(k + 1) * 384], start=k == 0, stop=k == 1)
                    else:
                        mm = pe.matmul(bank(i % 4), ckvT[:, t * P:(t + 1) * P], raw[:, slot, 768:1280], start=True, stop=True)
                    mm.then_inc(S[f"raw_done{slot}" if it["last"] else "up_done"], 1)

                def score(s):
                    h, q, br = s["h"], s["q"], s["br"]
                    pair = s["n"] % 2
                    if s["first"]:
                        pe.wait_ge(S["t_copied"], n("t_copied"))
                        pe.wait_ge(S["acc_copied"], n("acc_copied"))
                        pe.wait_ge(S["cache_loaded"], n("cache_loaded"))
                    pe.wait_ge(S["exp_done"], n("exp_done", -1))
                    if br == "A":
                        m = s["m"] * NH + h
                        tile, p0, kk = m // 2, m % 2 * HD, HD
                        qt, kt = qA[p0:p0 + kk, tile, :], kA[p0:p0 + kk, tile, :]
                    elif br == "B":
                        qt, kt = qB[0:QK, h % 4, :], kB[0:QK, h % 4, :]
                    else:
                        p0 = h // 4 * HD
                        qt, kt = qC[p0:p0 + HD, h % 4, :], kC[p0:p0 + HD, :]
                    qs = qt[:, q * P:(q + 1) * P]
                    if q == 0:
                        mm = pe.matmul(run(pair, 0, SEQ), qs, kt[:, 0:SEQ], start=True, stop=True)
                    else:
                        for out, c in halves(pair):
                            mm = pe.matmul(out, qs, kt[:, SEQ + c:SEQ + c + HALF], start=True, stop=True)
                    mm.then_inc(S["score_done"], 1)

                def turnp(s):
                    q, slot = s["q"], s["n"] % 4
                    if s["first"]:
                        pe.wait_ge(S["acc_copied"], n("acc_copied"))
                    pe.wait_ge(S["p_ready"], n("p_ready", -s["p_back"]))
                    pe.wait_ge(S["pt_copied"], n("pt_copied"))
                    for i in range(1 if q == 0 else NT):
                        mm = pe.transpose(line(2, P, off=i * P), prob[:, slot, i * P:(i + 1) * P], ident[:, :])
                    mm.then_inc(S["pt_done"], 1)

                def values(s):
                    h, br = s["h"], s["br"]
                    pe.wait_ge(S["pt_copied"], n("pt_copied"))
                    pe.wait_ge(S["gate_ready"], n("gate_ready"))
                    pe.wait_ge(S["ot_copied"], n("ot_copied"))
                    if br == "A":
                        p0, p1, v = 0, P, [vA[:, k, h * VD:(h + 1) * VD] for k in range(NK)]
                    elif br == "B":
                        p0, v = h % 2 * 64, [vB[:, k, h % 4, :] for k in range(NK)]
                    else:
                        p0, v = h % 2 * 64, [vC[:, k, h // 4 * 64:h // 4 * 64 + 64] for k in range(NK)]
                    p1 = p0 + (P if br == "A" else 64)
                    pe.matmul(line(3, SEQ, p0, p1, off=512 - SEQ), v[0], probTc[:, :], start=True, stop=True)
                    for k in range(NT):
                        mm = pe.matmul(line(3, DEC, p0, p1, off=512), v[k + 1], probT[:, k, :], start=k == 0, stop=k == NT - 1)
                    mm.then_inc(S["av_done"], 1)

                def ostat(s):
                    pe.wait_ge(S["osq_ready"], n("osq_ready", 1))
                    pe.wait_ge(S["gate_ready"], n("gate_ready"))
                    pe.wait_ge(S["ot_copied"], n("ot_copied"))
                    pe.wait_ge(S["on_ready"], n("on_ready"))
                    for t in range(NT):
                        mm = pe.matmul(bank(6)[:, t:t + 1], nsq[:, s["h"] % 2, t * P:(t + 1) * P], ones[:, 0:1],
                                       start=t == 0, stop=True, skip_group_check=True)
                    mm.then_inc(S["ostat_done"], 1)

                def obcast(s):
                    pe.wait_ge(S["gate_ready"], n("gate_ready"))
                    spread(3, diag[:, :, :], ("odiag_ready", n("odiag_ready")), "obc_done")

                do = dict(params=params, ada=ada, norm=norm, tm=tm, gate=gate, branch=branch, wo=wo, up=up, down=down,
                          turnc=turnc, turn=turn, upmm=upmm, score=score, turnp=turnp, values=values, ostat=ostat,
                          obcast=obcast)
                walk(pe, PLAN, do, lambda s: do[s["step"]](s), n)
            for t in range(NT):
                for j in range(2):
                    if t == j == 0:
                        pe.wait_ge(S["fm_read"], DEPTH * PER_LAYER["fm_read"] + CREDIT)
                    if 2 * t + j >= 4:
                        pe.wait_ge(S["y_copied"], 2 * t + j - 3)
                    for i in range(4):
                        mm = pe.transpose(bank((2 * t + j) % 4)[:, i * P:(i + 1) * P],
                                          xT[:, 4 * j + i, t * P:(t + 1) * P], ident[:, :])
                    mm.then_inc(S["y_turned"], 1)

        @block.scalar
        def _(act):
            act.wait_ge(S["c_turned"], 1)
            act.activation(cT[:, :, :].rearrange("p k j -> p j k"), bank(7, 2 * KD).rearrange("p (j k) -> p j k", j=2),
                           ACT.Silu).then_inc(S["c_ready"], 1)
            for t in range(NT):
                for j in range(2):
                    act.wait_ge(S["x_turned"], 2 * t + j + 1)
                    act.activation(xT[:, 4 * j:4 * j + 4, t * P:(t + 1) * P],
                                   bank((t * 2 + j) % 4).rearrange("p (i c) -> p i c", c=P), ACT.Copy).then_inc(S["x_copied"], 1)
            with act.Fori(0, DEPTH) as layer:
                n = Count(layer)

                def params(s):
                    act.wait_ge(S["rows_turned"], n("rows_turned", 1))
                    act.activation(PT[:, :], line(3, NPAR), ACT.Copy).then_inc(S["par_ready"], 1)
                    act.wait_ge(S["lam_step"], n("lam_step", 3))
                    act.activation(lame[:, :], lam2[:, :], ACT.Exp).then_inc(S["lam_exp"], 1)

                def norm(s):
                    act.wait_ge(S["fm_read"], n("fm_read"))
                    act.wait_ge(S["x_copied"], 2 * NT)
                    if s["which"]:
                        act.wait_ge(S["ctx_out"], n("ctx_out"))
                    for k in range(KD):
                        if k >= 2:
                            act.wait_ge(S["stat_done"], n("stat_done", k - 1))
                        act.activation(nsq[:, k % 2, :], xT[:, k, :], ACT.Square).then_inc(S["sq_ready"], 1)
                    for k in range(KD):
                        act.wait_ge(S["hf_ready"], n("hf_ready", k + 1))
                        act.activation(hhi[:, k, :], hf[:, k % 2, :], ACT.Copy).then_inc(S["hhi_ready"], 1)

                def split(s):
                    slot, sub, w = s["slot"], s["sub"], s["width"]
                    act.wait_ge(S[f"raw_full{slot}"], n(f"raw_full{slot}"))
                    act.wait_ge(S["sub_done"], n("sub_done", s["ahead"] - 1))
                    src, dst = sub_views(s)
                    act.activation(dst(whi), src, ACT.Copy).then_inc(S["hi_ready"], 1)

                def acc(s):
                    it = s["it"]
                    kind, t = it["kind"], it["tile"]
                    kt = key_tile(it)
                    if n.n.get("ctx_out"):
                        act.wait_ge(S["ctx_out"], n("ctx_out"))
                    if kind == "bc":
                        act.wait_ge(S["cache_loaded"], n("cache_loaded"))
                        act.wait_ge(S["sub_done"], n("sub_done"))
                    elif kind == "up":
                        name = f"raw_done{it['slot_raw']}" if it["last"] else "up_done"
                        act.wait_ge(S[name], n(name))
                    elif t < NT - 1:
                        act.wait_ge(S["acc_done"], n("acc_done", t + 2 - NT))
                    else:
                        act.wait_ge(S["sub_done"], n("sub_done"))
                    if kind in ("aq", "ak", "av", "cq", "ck", "bq") and it["groups"] and t == 0:
                        act.wait_ge(S["hlo_ready"], n("hlo_ready"))
                    b = it["bank"]
                    st = stage[:, it["slot"], :] if it["groups"] else None
                    if kind in ("aq", "ak"):
                        act.activation(st, bank(b), ACT.Copy).then_inc(S["acc_copied"], 1)
                    elif kind == "cq":
                        act.activation(st.rearrange("p (r g d) -> p r g d", r=4, g=2),
                                       bank(b).rearrange("p (g r d) -> p r g d", r=4, g=2), ACT.Copy).then_inc(S["acc_copied"], 1)
                    elif kind == "av":
                        act.activation(vA[:, kt, :], bank(b), ACT.Copy).then_inc(S["acc_copied"], 1)
                        if t == 0:
                            act.wait_ge(S["acc_copied"], n("acc_copied", 1))
                            act.dma_start(new_dv[0, ds(layer, 1)].rearrange("l p h d -> p (l h d)"), vA[:, 0, :])\
                               .then_inc(S["ctx_out"], 16)
                    elif kind == "ck":
                        act.activation(st[:, 0:P], bank(b)[:, 0:P], ACT.Copy)
                        act.activation(vC[:, kt, :], bank(b)[:, P:2 * P], ACT.Copy).then_inc(S["acc_copied"], 1)
                        if t == 0:
                            act.wait_ge(S["acc_copied"], n("acc_copied", 1))
                            act.dma_start(new_gv[0, ds(layer, 1)].rearrange("l p h d -> p (l h d)"), vC[:, 0, :])\
                               .then_inc(S["ctx_out"], 16)
                    elif kind == "bq":
                        act.activation(kpe[:, kt, :], bank(b)[:, QR + KVR:BW], ACT.Copy)
                        if t == 0:
                            act.activation(ckv_out[:, :], bank(b)[:, QR:BW], ACT.Copy)
                        act.activation(st[:, 0:QR + KVR], bank(b)[:, 0:QR + KVR], ACT.Copy).then_inc(S["acc_copied"], 1)
                        if t == 0:
                            act.wait_ge(S["acc_copied"], n("acc_copied", 1))
                            act.dma_start(new_ckv[0, ds(layer, 1)].rearrange("l p d -> p (l d)"), ckv_out[:, 0:KVR])\
                               .then_inc(S["ctx_out"], 16)
                            act.dma_start(new_kpe[0, ds(layer, 1)].rearrange("l p d -> p (l d)"), ckv_out[:, KVR:])\
                               .then_inc(S["ctx_out"], 16)
                    elif kind == "bc":
                        act.activation(kpe[:, 1, :], cached[:, KVR:KVR + ROPE], ACT.Copy)
                        act.activation(st[:, QR:QR + KVR], cached[:, 0:KVR], ACT.Copy).then_inc(S["acc_copied"], 1)
                    elif it["q"]:
                        act.activation(st[:, 0:4 * QK], bank(b, 4 * QK), ACT.Copy).then_inc(S["acc_copied"], 1)
                    else:
                        heads = st[:, 0:4 * QK].rearrange("p (h d) -> p h d", h=4)
                        kv = bank(b).rearrange("p (h d) -> p h d", h=4)
                        act.activation(heads[:, :, 0:NOPE], kv[:, :, 0:NOPE], ACT.Copy)
                        act.activation(heads[:, :, NOPE:QK], kpe[:, t, :].unsqueeze(1).to_broadcast([P, 4, ROPE]), ACT.Copy)
                        act.activation(vB[:, t, :, :], kv[:, :, NOPE:], ACT.Copy).then_inc(S["acc_copied"], 1)

                def turn(s):
                    it = s["it"]
                    kind, t, k = it["kind"], it["tile"], key_tile(it)
                    act.wait_ge(S["t_done"], n("t_done", 1))
                    b5 = bank(5).rearrange("p (i c) -> p i c", c=P)
                    q, k = slice(t * P, (t + 1) * P), slice(k * P, (k + 1) * P)
                    if kind == "bq":
                        act.activation(bqT[:, :, q], b5[:, 0:2, :], ACT.Copy)
                        act.activation(ckvT[:, k], b5[:, 2, :], ACT.Copy).then_inc(S["t_copied"], 1)
                    else:
                        out = {"aq": lambda: qA[:, :, q], "ak": lambda: kA[:, :, k], "cq": lambda: qC[:, :, q],
                               "ck": lambda: kC[:, k], "bc": lambda: ckvT[:, k],
                               "up": lambda: (qB[0:QK, :, q] if it.get("q") else kB[0:QK, :, k])}[kind]()
                        src = {"ck": b5[:, 0, :], "bc": b5[:, 0, :], "up": b5[0:QK, :, :]}.get(kind, b5)
                        act.activation(out, src, ACT.Copy).then_inc(S["t_copied"], 1)
                    if t == 0 and kind == "ak":
                        act.dma_start(new_dk[0, ds(layer, 1)].rearrange("l p m h d -> p (l m h d)"), stage[:, it["slot"], :])\
                           .then_inc(S["ctx_out"], 16)
                    if t == 0 and kind == "ck":
                        act.dma_start(new_gk[0, ds(layer, 1)].rearrange("l p h d -> p (l h d)"), stage[:, it["slot"], 0:P])\
                           .then_inc(S["ctx_out"], 16)

                def turnc(s):
                    act.wait_ge(S["t_done"], n("t_done", 1))
                    if s["b"] == 0:
                        act.activation(kA[:, :, P:2 * P], bank(5).rearrange("p (i c) -> p i c", c=P), ACT.Copy)\
                           .then_inc(S["t_copied"], 1)
                    else:
                        act.activation(kC[:, P:2 * P], bank(5, P), ACT.Copy).then_inc(S["t_copied"], 1)

                def gate(s):
                    slot = s["g"] % GATE_SLOTS
                    act.wait_ge(S["sub_done"], n("sub_done", 1))
                    act.wait_ge(S["fm_read"], n("fm_read"))
                    act.wait_ge(S["mg_ready"], n("mg_ready"))
                    act.activation(gated[:, slot, :], run(3), ACT.Tanh, scale=0.5).then_inc(S["gate_ready"], 1)

                def score(s):
                    if s["first"]:
                        act.wait_ge(S["ctx_out"], n("ctx_out"))
                    act.wait_ge(S["max_ready"], n("max_ready", 1))
                    slot, pair = s["n"] % 4, s["n"] % 2
                    w = SEQ if s["q"] == 0 else T
                    act.activation(prob[:, slot, 0:w], run(pair, 0, w), ACT.Exp, bias=negmax[:, slot:slot + 1],
                                   accum_out=den[:, slot:slot + 1]).then_inc(S["exp_done"], 1)

                def turnp(s):
                    q = s["q"]
                    act.wait_ge(S["pt_done"], n("pt_done", 1))
                    act.wait_ge(S["av_done"], n("av_done"))
                    if q == 0:
                        act.activation(probTc[:, :], line(2, P), ACT.Copy).then_inc(S["pt_copied"], 1)
                    else:
                        act.activation(probT[:, :, (q - 1) * P:q * P], line(2).rearrange("p (k c) -> p k c", c=P), ACT.Copy)\
                           .then_inc(S["pt_copied"], 1)

                def cache(s):
                    act.wait_ge(S["olo_ready"], n("olo_ready"))
                    act.wait_ge(S["ohi_ready"], n("ohi_ready"))
                    act.wait_ge(S["av_done"], n("av_done"))
                    act.wait_ge(S["hlo_ready"], n("hlo_ready"))
                    one = ds(layer, 1)
                    if s["b"] == 0:
                        act.dma_start(cached[:, 0:512], cache_dk[0, one].rearrange("l p m h d -> p (l m h d)"))\
                           .then_inc(S["cache_loaded"], 16)
                        act.dma_start(vA[:, 1, :], cache_dv[0, one].rearrange("l p h d -> p (l h d)"))\
                           .then_inc(S["cache_loaded"], 16)
                    elif s["b"] == 1:
                        act.dma_start(cached[:, 0:KVR], cache_ckv[0, one].rearrange("l p d -> p (l d)"))\
                           .then_inc(S["cache_loaded"], 16)
                        act.dma_start(cached[:, KVR:KVR + ROPE], cache_kpe[0, one].rearrange("l p d -> p (l d)"))\
                           .then_inc(S["cache_loaded"], 16)
                    else:
                        act.dma_start(cached[:, 0:P], cache_gk[0, one].rearrange("l p h d -> p (l h d)"))\
                           .then_inc(S["cache_loaded"], 16)
                        act.dma_start(vC[:, 1, :], cache_gv[0, one].rearrange("l p h d -> p (l h d)"))\
                           .then_inc(S["cache_loaded"], 16)

                def osplit(s):
                    act.wait_ge(S["on_ready"], n("on_ready"))
                    act.wait_ge(S["ot_copied"], n("ot_copied"))
                    for k in range(4):
                        act.activation(ohi[:, k, :], oT[:, k, :], ACT.Copy).then_inc(S["ohi_ready"], 1)

                def msplit(s):
                    act.wait_ge(S["mg_ready"], n("mg_ready"))
                    for k in range(KD):
                        act.activation(hhi[:, k, :], merged[:, k, :], ACT.Copy, scale=0.5).then_inc(S["mhi_ready"], 1)

                def up_out(s):
                    u = n.turn * 2 + s["a"] + s["f0"]
                    act.wait_ge(S["sub_done"], n("sub_done"))
                    act.wait_ge(S["alo_ready"], n("alo_ready", -1))
                    for j, v in enumerate((va, vg)):
                        act.activation(v[:, s["s"], :], run(2 * s["s"] + j), ACT.Identity,
                                       scale=PT[:, ds(u + (P_W + 44 + j * FT), 1)], bias=PT[:, ds(u + (P_CB + j * FT), 1)])\
                           .then_inc(S["v_ready"], 1)

                def up_out2(s):
                    act.wait_ge(S["fm_read"], n("fm_read"))
                    act.activation(vg[:, s["s"], :], vg[:, s["s"], :], ACT.Silu).then_inc(S["silu_done"], 1)
                    act.wait_ge(S["prod_ready"], n("prod_ready", 1))
                    act.activation(ahi[:, ds(n.turn * 2 + s["a"], 1), :], va[:, s["s"], :].unsqueeze(1), ACT.Copy)\
                       .then_inc(S["ahi_ready"], 1)

                do = dict(params=params, norm=norm, split=split, acc=acc, turn=turn, turnc=turnc, gate=gate, score=score,
                          turnp=turnp, osplit=osplit, msplit=msplit, up_out=up_out,
                          up_out2=up_out2, cache=cache)
                walk(act, PLAN, do, lambda s: do[s["step"]](s), n)
            for i in range(2 * NT):
                act.wait_ge(S["y_turned"], i + 1)
                act.activation(xin[:, i // 2, i % 2 * 512:(i % 2 + 1) * 512], bank(i % 4), ACT.Copy).then_inc(S["y_copied"], 1)

        @block.vector
        def _(dve):
            dve.wait_ge(S["const_set"], 4)
            dve.wait_ge(S["const_loaded"], 80)
            with dve.Fori(0, DEPTH) as layer:
                n = Count(layer)

                def params(s):
                    dve.wait_ge(S["gains_loaded"], n("gains_loaded", 16 * 7))
                    for g, w, by in ((G_DQ, HD, HD ** -0.5), (G_GQ, HD, HD ** -0.5), (G_MQ, QK, QK ** -0.5)):
                        dve.tensor_scalar(gains[:, g:g + w], gains[:, g:g + w], by, None, ALU.mult).then_inc(S["gain_ready"], 1)
                    dve.tensor_tensor(lamv[:, 0, :], lamv[:, 0, :], lamv[:, 1, :], ALU.mult).then_inc(S["lam_step"], 1)
                    dve.tensor_tensor(lamv[:, 2, :], lamv[:, 2, :], lamv[:, 3, :], ALU.mult).then_inc(S["lam_step"], 1)
                    dve.wait_ge(S["lam_step"], n("lam_step", 2))
                    dve.tensor_reduce(lam2[:, :], lamv[:, 0:4:2, :], AX.X, ALU.add).then_inc(S["lam_step"], 1)
                    dve.wait_ge(S["lam_exp"], n("lam_exp", 1))
                    dve.scalar_tensor_tensor(out=neglam[:, :], in0=lame[:, 1:2], scalar=gains[:, G_LC:G_LC + 1],
                                             in1=lame[:, 0:1], op0=ALU.subtract, op1=ALU.subtract).then_inc(S["lam_step"], 1)
                    dve.wait_ge(S["par_ready"], n("par_ready", 1))
                    dve.tensor_tensor(dgain[:, :], PT[:, P_DN:P_DN + 1], gains[:, G_LC + 1:G_LC + 2], ALU.mult)\
                       .then_inc(S["lam_step"], 1)

                def modulation(s):
                    for slot in range(2):
                        dve.wait_ge(S[f"raw_done{slot}"], n(f"raw_done{slot}"))
                    dve.tensor_tensor(mod[:, :, :], bank(7, 96).rearrange("p (t j) -> p t j", j=2),
                                      PT[:, 0:48].unsqueeze(2).to_broadcast([P, 48, 2]), ALU.add).then_inc(S["mod_ready"], 1)
                    dve.wait_ge(S["mod_ready"], n("mod_ready", 1))
                    for i, (g, t) in enumerate(((P_NM, KD), (P_NF, 4 * KD))):
                        dve.scalar_tensor_tensor(out=scale[:, i, :, :], in0=mod[:, t:t + KD, :], scalar=1.0,
                                                 in1=PT[:, g:g + KD].unsqueeze(2).to_broadcast([P, KD, 2]),
                                                 op0=ALU.add, op1=ALU.mult).then_inc(S["mod_ready"], 1)
                    dve.wait_ge(S["mod_ready"], n("mod_ready", 3))

                def norm(s):
                    w = s["which"]
                    dve.wait_ge(S["stat_done"], n("stat_done", KD))
                    dve.tensor_scalar(nmean[:, :], bank(6, NT), 1.0 / D, EPS, ALU.mult, ALU.add).then_inc(S["nms_ready"], 1)
                    dve.wait_ge(S["bc_done"], n("bc_done", 1))
                    for k in range(KD):
                        if k >= 2:
                            dve.wait_ge(S["hlo_ready"], n("hlo_ready", k - 1))
                        h = hf[:, k % 2, :]
                        dve.tensor_tensor(h, xT[:, k, :], run(0), ALU.mult).then_inc(S["xn_done"], 1)
                        dve.wait_ge(S["xn_done"], n("xn_done", k + 1))
                        for j, (a, b) in enumerate(((0, SEQ), (SEQ, T))):
                            ins = dve.tensor_scalar(h[:, a:b], h[:, a:b], scale[:, w, k, j:j + 1],
                                                    mod[:, 3 * KD * w + k, j:j + 1], ALU.mult, ALU.add)
                        ins.then_inc(S["hf_ready"], 1)

                def split(s):
                    dve.wait_ge(S["hi_ready"], n("hi_ready", 1))
                    src, dst = sub_views(s)
                    name = f"raw_done{s['slot']}" if s["last"] else "lo_ready"
                    dve.tensor_tensor(dst(wlo), src, dst(whi).bitcast(F32), ALU.subtract).then_inc(S[name], 1)

                before = []

                def finish():
                    if before:
                        it, gained, cos, sin = before.pop()
                        r0, half, x, cs, tc, ts = rope_views(it)
                        dve.wait_ge(S["gained"], gained)
                        dve.tensor_tensor(tc, x, cs[0], ALU.mult).then_inc(S["cos_done"], 1)
                        dve.wait_ge(S["cos_done"], cos)
                        dve.wait_ge(S["sin_ready"], sin)
                        dve.tensor_tensor(x, tc, ts, ALU.add).then_inc(S["item_ready"], 1)

                def tick(s):
                    it = s["it"]
                    a, b = span(it)
                    st = stage[:, it["slot"], :]
                    par, heads = it["par"], sum(g[1] for g in it["groups"])
                    dve.wait_ge(S["acc_copied"], n("acc_copied", -s["acc_back"]))
                    dve.tensor_tensor(tmpq[:, a:b], st[:, a:b], st[:, a:b], ALU.mult).then_inc(S["sqr_done"], 1)
                    dve.wait_ge(S["sqr_done"], n("sqr_done", 1))
                    h0 = 0
                    for c, nh, dh in it["groups"]:
                        dve.tensor_reduce(ssum[:, par, h0:h0 + nh], tmpq[:, c:c + nh * dh].rearrange("p (h d) -> p h d", h=nh),
                                          AX.X, ALU.add).then_inc(S["ss_ready"], 1)
                        h0 += nh
                    dve.wait_ge(S["ss_ready"], n("ss_ready", len(it["groups"])))
                    h0 = 0
                    for c, nh, dh in it["groups"]:
                        dve.tensor_scalar(smean[:, par, h0:h0 + nh], ssum[:, par, h0:h0 + nh], 1.0 / dh, EPS,
                                          ALU.mult, ALU.add).then_inc(S["ms_done"], 1)
                        h0 += nh
                    finish()
                    dve.wait_ge(S["rstd_ready"], n("rstd_ready", 1))
                    h0 = 0
                    for c, nh, dh in it["groups"]:
                        x = st[:, c:c + nh * dh].rearrange("p (h d) -> p h d", h=nh)
                        ins = dve.tensor_tensor(x, x, rstd[:, par, h0:h0 + nh].unsqueeze(2).to_broadcast([P, nh, dh]), ALU.mult)
                        h0 += nh
                    ins.then_inc(S["xh_ready"], 1)
                    if it["rope"]:
                        before.append((it, n("gained", 1), n("cos_done", 1), n("sin_ready", 1)))
                    else:
                        dve.wait_ge(S["xh_ready"], n("xh_ready", 1))
                        for g, (c, nh, dh) in zip(it["gains"], it["groups"]):
                            x = st[:, c:c + nh * dh].rearrange("p (h d) -> p h d", h=nh)
                            ins = dve.tensor_tensor(x, x, gains[:, g:g + dh].unsqueeze(1).to_broadcast([P, nh, dh]), ALU.mult)
                        ins.then_inc(S["item_ready"], 1)

                def flush(s):
                    finish()

                def score(s):
                    slot, pair = s["n"] % 4, s["n"] % 2
                    dve.wait_ge(S["score_done"], n("score_done", 1))
                    dve.tensor_reduce(negmax[:, slot:slot + 1], run(pair, 0, SEQ if s["q"] == 0 else T), AX.X, ALU.max,
                                      negate=True).then_inc(S["max_ready"], 1)

                def soft(s):
                    a = s["n"] % 4
                    w = SEQ if s["q"] == 0 else T
                    k = 2 if s["br"] == "A" else 1
                    dve.wait_ge(S["exp_done"], n("exp_done", -s["back"]))
                    dve.reciprocal(rden[:, a:a + k], den[:, a:a + k]).then_inc(S["rden_done"], 1)
                    dve.wait_ge(S["rden_done"], n("rden_done", 1))
                    if k == 1:
                        dve.tensor_scalar(prob[:, a, 0:w], prob[:, a, 0:w], rden[:, a:a + 1], None, ALU.mult)\
                           .then_inc(S["p_ready"], 1)
                    else:
                        dve.tensor_scalar(prob[:, a + 1, 0:w], prob[:, a + 1, 0:w], rden[:, a + 1:a + 2], neglam[:, 0:1],
                                          ALU.mult, ALU.mult).then_inc(S["p1_done"], 1)
                        dve.wait_ge(S["p1_done"], n("p1_done", 1))
                        dve.scalar_tensor_tensor(out=prob[:, a, 0:w], in0=prob[:, a, 0:w], scalar=rden[:, a:a + 1],
                                                 in1=prob[:, a + 1, 0:w], op0=ALU.mult, op1=ALU.add).then_inc(S["p_ready"], 1)

                def values(s):
                    h = s["h"]
                    dve.wait_ge(S["av_done"], n("av_done", 1))
                    p0, p1, tile = (0, P, h) if s["br"] == "A" else (h % 2 * 64, h % 2 * 64 + 64, h // 2)
                    dve.tensor_copy(oT[p0:p1, tile, :], line(3, T, p0, p1, off=512 - SEQ)).then_inc(S["ot_copied"], 1)

                def ostat(s):
                    dve.wait_ge(S["ostat_done"], n("ostat_done", 1))
                    dve.tensor_scalar(nmean[:, :], bank(6, NT), 1.0 / VD, EPS, ALU.mult, ALU.add).then_inc(S["oms_ready"], 1)

                def obcast(s):
                    dve.wait_ge(S["obc_done"], n("obc_done", 1))
                    dve.scalar_tensor_tensor(out=oT[:, s["h"], :], in0=oT[:, s["h"], :], scalar=dgain[:, 0:1], in1=run(3),
                                             op0=ALU.mult, op1=ALU.mult).then_inc(S["on_ready"], 1)

                def osplit(s):
                    for k in range(4):
                        dve.wait_ge(S["ohi_ready"], n("ohi_ready", k + 1))
                        dve.tensor_tensor(olo[:, k, :], oT[:, k, :], ohi[:, k, :].bitcast(F32), ALU.subtract)\
                           .then_inc(S["olo_ready"], 1)

                def merge(s):
                    dve.wait_ge(S["sub_done"], n("sub_done"))
                    dve.wait_ge(S["gate_ready"], n("gate_ready"))
                    for j in range(2):
                        i = 2 * s["k"] + j
                        g = gated[:, i % GATE_SLOTS, :]
                        dve.scalar_tensor_tensor(out=g if s["b"] else merged[:, i, :], in0=g, scalar=1.0, in1=run(i % 3),
                                                 op0=ALU.add, op1=ALU.mult).then_inc(S["fm_read"], 1)

                def msplit(s):
                    for k in range(KD):
                        dve.wait_ge(S["mhi_ready"], n("mhi_ready", k + 1))
                        dve.scalar_tensor_tensor(out=hlo[:, k, :], in0=merged[:, k, :], scalar=0.5,
                                                 in1=hhi[:, k, :].bitcast(F32), op0=ALU.mult, op1=ALU.subtract)\
                           .then_inc(S["mlo_ready"], 1)

                def residual(f, pair, m0):
                    for j, (a, b) in enumerate(((0, SEQ), (SEQ, T))):
                        x = xT[:, ds(f, 1), a:b]
                        ins = dve.scalar_tensor_tensor(out=x, in0=run(pair, a, b).unsqueeze(1), scalar=mod[:, ds(f + m0, 1), j],
                                                       in1=x, op0=ALU.mult, op1=ALU.add)
                    ins.then_inc(S["fm_read"], 1)

                def wo_out(s):
                    dve.wait_ge(S["sub_done"], n("sub_done"))
                    for j in range(2):
                        residual((n.turn * 2 + s["a"]) * 2 + j, 2 * s["s"] + j, 2 * KD)

                def down_out(s):
                    dve.wait_ge(S["sub_done"], n("sub_done"))
                    residual(n.turn * 2 + s["a"], 2 * s["s"], 5 * KD)

                def up_out(s):
                    u = n.turn * 2 + s["a"] + s["f0"]
                    for j, v in enumerate((va, vg)):
                        v = v[:, s["s"], :]
                        pair = 2 * s["s"] + j
                        dve.wait_ge(S["v_ready"], n("v_ready", j + 1))
                        for a, b in ((0, SEQ), (SEQ, T)):
                            ins = dve.scalar_tensor_tensor(out=v[:, a + 1:b], in0=run(pair, a, b - 1),
                                                           scalar=PT[:, ds(u + (P_W + j * FT), 1)], in1=v[:, a + 1:b],
                                                           op0=ALU.mult, op1=ALU.add)
                        ins.then_inc(S["tap_done"], 1)
                        dve.wait_ge(S["tap_done"], n("tap_done", j + 1))
                        for a, b in ((0, SEQ), (SEQ, T)):
                            ins = dve.scalar_tensor_tensor(out=v[:, a:b - 1], in0=run(pair, a + 1, b),
                                                           scalar=PT[:, ds(u + (P_W + 88 + j * FT), 1)], in1=v[:, a:b - 1],
                                                           op0=ALU.mult, op1=ALU.add)
                        ins.then_inc(S["fm_read"], 1)

                do = dict(params=params, mod=modulation, norm=norm, split=split, tick=tick, flush=flush, score=score,
                          soft=soft, values=values, ostat=ostat, obcast=obcast, osplit=osplit, merge=merge,
                          msplit=msplit, wo_out=wo_out, down_out=down_out, up_out=up_out)
                walk(dve, PLAN, do, lambda s: do[s["step"]](s), n)

        @block.gpsimd
        def _(pool):
            pool.memset(ones[:, :], 1.0).then_inc(S["const_set"], 1)
            pool.memset(mhalf[:, :], -0.5).then_inc(S["const_set"], 1)
            pool.memset(epsc[:, :], EPS).then_inc(S["const_set"], 1)
            for name in PER_LAYER:
                if name not in DMA_SEMS:
                    pool.sem_inc(S[name], CREDIT)
            pool.wait_ge(S["const_set"], 3)
            pool.memset(epsc[:, :], EPS).then_inc(S["const_set"], 1)
            pool.wait_ge(S["const_loaded"], 80)
            with pool.Fori(0, DEPTH) as layer:
                n = Count(layer)

                def diagonals(signal):
                    for t in range(NT):
                        pool.tensor_tensor(diag[:, t, :], ident[:, :], nrstd[:, t:t + 1].to_broadcast([P, P]), ALU.mult)\
                            .then_inc(S[signal], 1)

                def norm(s):
                    pool.wait_ge(S["nms_ready"], n("nms_ready", 1))
                    pool.tensor_tensor(nrstd[:, :], nmean[:, :], mhalf[:, 0:NT], ALU.pow).then_inc(S["nrs_ready"], 1)
                    pool.wait_ge(S["nrs_ready"], n("nrs_ready", 1))
                    diagonals("diag_ready")
                    for k in range(KD):
                        pool.wait_ge(S["hhi_ready"], n("hhi_ready", k + 1))
                        pool.tensor_tensor(hlo[:, k, :], hf[:, k % 2, :], hhi[:, k, :].bitcast(F32), ALU.subtract)\
                            .then_inc(S["hlo_ready"], 1)

                def tick(s):
                    it = s["it"]
                    par, heads = it["par"], sum(g[1] for g in it["groups"])
                    pool.wait_ge(S["ms_done"], n("ms_done", len(it["groups"])))
                    pool.tensor_tensor(rstd[:, par, 0:heads], smean[:, par, 0:heads], mhalf[:, 0:heads], ALU.pow)\
                        .then_inc(S["rstd_ready"], 1)
                    if not it["rope"]:
                        return
                    c, nh, dh = it["groups"][0]
                    g = it["gains"][0]
                    x = stage[:, it["slot"], 0:nh * dh].rearrange("p (h d) -> p h d", h=nh)
                    pool.wait_ge(S["xh_ready"], n("xh_ready", 1))
                    pool.tensor_tensor(x, x, gains[:, g:g + dh].unsqueeze(1).to_broadcast([P, nh, dh]), ALU.mult)\
                        .then_inc(S["gained"], 1)
                    pool.wait_ge(S["gained"], n("gained", 1))
                    pool.wait_ge(S["item_ready"], n("item_ready"))
                    r0, half, x, cs, tc, ts = rope_views(it)
                    sn = cs[1]
                    pool.tensor_tensor(ts[:, :, 0:half], x[:, :, half:], sn[:, :, 0:half], ALU.mult)
                    pool.tensor_tensor(ts[:, :, half:], x[:, :, 0:half], sn[:, :, half:], ALU.mult).then_inc(S["sin_ready"], 1)

                def ostat(s):
                    pool.wait_ge(S["ot_copied"], n("ot_copied"))
                    pool.wait_ge(S["ostat_done"], n("ostat_done"))
                    h = s["h"]
                    pool.tensor_tensor(nsq[:, h % 2, :], oT[:, h, :], oT[:, h, :], ALU.mult).then_inc(S["osq_ready"], 1)
                    pool.wait_ge(S["oms_ready"], n("oms_ready", 1))
                    pool.tensor_tensor(nrstd[:, :], nmean[:, :], mhalf[:, 0:NT], ALU.pow).then_inc(S["ors_ready"], 1)
                    pool.wait_ge(S["ors_ready"], n("ors_ready", 1))
                    pool.wait_ge(S["obc_done"], n("obc_done"))
                    diagonals("odiag_ready")

                def merge(s):
                    if s["b"]:
                        for j in range(2):
                            i = 2 * s["k"] + j
                            pool.wait_ge(S["fm_read"], n("fm_read", j + 1))
                            pool.tensor_tensor(merged[:, i, :], merged[:, i, :], gated[:, i % GATE_SLOTS, :], ALU.add)\
                                .then_inc(S["mg_ready"], 1)

                def up_out2(s):
                    pool.wait_ge(S["silu_done"], n("silu_done", 1))
                    a = va[:, s["s"], :]
                    pool.tensor_tensor(a, a, vg[:, s["s"], :], ALU.mult).then_inc(S["prod_ready"], 1)
                    pool.wait_ge(S["ahi_ready"], n("ahi_ready", 1))
                    u = ds(n.turn * 2 + s["a"], 1)
                    pool.tensor_tensor(alo[:, u, :], a.unsqueeze(1), ahi[:, u, :].bitcast(F32), ALU.subtract)\
                        .then_inc(S["alo_ready"], 1)

                do = dict(norm=norm, tick=tick, ostat=ostat, merge=merge, up_out2=up_out2)
                walk(pool, PLAN, do, lambda s: do[s["step"]](s), n)


_INS = ["x_prompt", "x_sample", "c", "cache_diff_k", "cache_diff_v", "cache_mla_ckv", "cache_mla_kpe", "cache_gqa_k",
        "cache_gqa_v", "c_ctx", "w_ada", "b_ada", "norm_mix", "w_in", "diff_qk_norm", "diff_lambda", "diff_out_norm",
        "mla_q_norm", "w_mla_q_up", "mla_kv_norm", "w_mla_kv_up", "mla_qk_norm", "gqa_qk_norm", "w_branch_a",
        "w_branch_b", "w_branch_c", "w_o", "norm_ffn", "w_up", "conv_w", "conv_b", "w_down"]
_OUTS = [(1, SEQ, D), (1, DEC, D), (1, DEPTH, SEQ, 2, NH, HD), (1, DEPTH, SEQ, NH, VD), (1, DEPTH, SEQ, KVR),
         (1, DEPTH, SEQ, ROPE), (1, DEPTH, SEQ, GKV, HD), (1, DEPTH, SEQ, GKV, HD)]


def rope_table(dim):
    t = np.arange(DEC, dtype=np.float32)
    quarter = dim // 4
    inv = (np.float32(1.0) / np.float32(BASE) ** (np.arange(quarter, dtype=np.float32) / np.float32(quarter))).astype(np.float32)
    ang = np.concatenate([(t // GRID_W)[:, None] * inv, (t % GRID_W)[:, None] * inv], axis=-1).astype(np.float32)
    cos, sin = np.cos(ang), np.sin(ang)
    both = np.stack([np.concatenate([cos, cos], -1), np.concatenate([-sin, sin], -1)], 1).astype(np.float32)
    return np.ascontiguousarray(both.reshape(DEC // P, P, 2, dim).transpose(1, 0, 2, 3))


def layer_constants():
    lam = [0.8 - 0.6 * math.exp(-0.3 * layer) for layer in range(DEPTH)]
    return np.array([[x, 1.0 - x] for x in lam], dtype=np.float32)


def kernel(**inputs):
    import concourse.bacc as _bacc
    from concourse.bass_utils import run_bass_kernel_spmd as _run

    nc = _bacc.Bacc("TRN2", target_bir_lowering=False, num_devices=1)
    arrays, args = {}, []
    for name in _INS:
        arrays[f"in_{name}"] = np.ascontiguousarray(inputs[name])
    arrays["const_ident"] = np.eye(P, dtype=np.float32)
    arrays["const_rope_h"] = rope_table(HD)
    arrays["const_rope_r"] = rope_table(ROPE)
    arrays["const_layer"] = layer_constants()
    for name, a in arrays.items():
        args.append(nc.dram_tensor(name, a.shape, F32, kind="ExternalInput").ap())
    for i, shape in enumerate(_OUTS):
        args.append(nc.dram_tensor(f"out_{i}", shape, F32, kind="ExternalOutput").ap())
    program(nc, *args)
    r = _run(nc, [arrays], core_ids=[0])
    return tuple(r.results[0][f"out_{i}"] for i in range(len(_OUTS)))
```

```python
import math
from contextlib import ExitStack

import numpy as np

import concourse.bass as bass
from concourse import mybir

F32 = mybir.dt.float32
F32R = mybir.dt.float32r
ALU = mybir.AluOpType
ACT = mybir.ActivationFunctionType
AX = mybir.AxisListType
ds = bass.ds

P = 128
D, DEPTH, SEQ, DEC, PAST = 1024, 2, 128, 512, 128
HD, NH, VD = 64, 4, 128
QR, KVR, NOPE, ROPE, MH = 256, 128, 64, 32, 8
QK = NOPE + ROPE
GH, GKV = 8, 2
FF = 2816
EPS = 1e-6
GRID_W, BASE = 64, 10000.0
T = SEQ + DEC
NT = T // P
KEYS = SEQ + PAST + DEC
NK = KEYS // P
KD = D // P
HALF = T // 2
OFF = 512 - HALF
FT = FF // P
FPARTS = [(0, 12), (12, 10)]
SUB = 1024
AQ, AK, AV, BQ, BKV, CQ, CK, GATE = 0, 512, 1024, 1536, 1792, 1952, 2464, 2720
BW = QR + KVR + ROPE
P_ADA, P_NM, P_NF, P_CB, P_DN, P_W = 0, 48, 56, 64, 108, 109
NPAR = 109 + 3 * 44
G_DQ, G_DK, G_GQ, G_GK, G_MQ, G_MK, G_BQ, G_BKV, G_LC = 0, 64, 128, 192, 256, 352, 448, 704, 832
NGAIN = 834
GATE_SLOTS = 6
ADA_FIRST = 2 * KD
ADA_EARLY = 2
ADA_AT = 8


def build_plan():
    plan = []
    pending = []
    order = []
    count = dict(unit=0, split=0, gemm=0, item=0, score=0, gate=0, ada_unit=0, ada=0, ada_turn=0)
    at = dict(slot=0, held=None, turned=5)

    def add(kind, **k):
        plan.append(dict(step=kind, **k))

    def queue(src, widths, **k):
        for j, w in enumerate(widths):
            pending.append((src if j == 0 else None, w, sum(widths[:j]), j == len(widths) - 1, k))
            order.append(src)

    def prefetch(ahead):
        while pending and count["split"] < count["gemm"] + ahead:
            src, w, off, last, k = pending.pop(0)
            cols = k.get("cols")
            if src == "ada_first":
                at["slot"] = 2 + k["u"]
            elif src:
                count["unit"] += count["unit"] % 2 == at["held"]
                at["slot"] = count["unit"] % 2
                add("unit", src=src, slot=at["slot"], a=0, **k)
                count["unit"] += 1
            add("split", slot=at["slot"], sub=count["split"] % 2, off=off, width=w, last=last, cols=cols)
            count["split"] += 1

    def gemm(kind, **k):
        prefetch(2)
        assert order.pop(0).startswith(kind)
        add(kind, sub=count["gemm"] % 2, **k)
        count["gemm"] += 1

    def queue_ada(n):
        for _ in range(n):
            queue("ada" if count["ada_unit"] >= ADA_FIRST // 2 else "ada_first", [SUB] * 2, u=count["ada_unit"])
            count["ada_unit"] += 1

    def ada(n=1):
        for _ in range(n):
            for part in ada_parts():
                part()

    def ada_parts():
        def last():
            gemm("ada", j=1)
            ada_turn()
            add("ada_row", u=count["ada"])
            count["ada"] += 1
        return [lambda: prefetch(2), lambda: gemm("ada", j=0), last]

    def ada_turn():
        if count["ada"] > count["ada_turn"]:
            add("ada_turn", u=count["ada_turn"])
            count["ada_turn"] += 1

    def queue_tm(col, w):
        for u in range(2):
            queue("tm", [2 * w] * 2, col=col, w=w, u=u)

    def queue_gates(b, first, n):
        for u in range(n):
            queue("gate", [SUB] * 2, col=GATE + b * D + (first + 2 * u) * P, cols=(KD, P))

    def gate_parts(n=4):
        def part(i):
            ks = range(i * KD // n, (i + 1) * KD // n)
            if i < n - 1:
                prefetch(2)
                add("gate_part", ks=ks, sub=count["gemm"] % 2)
            else:
                gemm("gate", g=count["gate"] % KD, ks=ks)
                count["gate"] += 1
        return [lambda i=i: part(i) for i in range(n)]

    def gate():
        for part in gate_parts(1):
            part()

    def item(kind, width, groups, gains, rope, tile, **k):
        it = dict(kind=kind, width=width, groups=groups, gains=gains, rope=rope, tile=tile, bank=tile, **k)
        if groups:
            it["slot"], it["par"] = count["item"] % 5, count["item"] % 2
            count["item"] += 1
        return it

    def turn(it, other):
        at["turned"] = bank = other if at["turned"] == 5 else 5
        add("turn", it=it, bank=bank)

    def turn_cache(b):
        add("turnc", b=b)
        at["turned"] = 5

    def chunk(w, first, prev):
        for i, it in enumerate(prev):
            add("acc", it=it)
            if i == 1:
                prefetch(2)
        for s in range(4):
            gemm("tm", w=w, s=s, first=first, after_norm=first and w == 512)
            for it in prev[2 * s:2 * s + 2]:
                add("tick", it=it)
            if s == 2 and prev:
                add("flush")
            if s >= 1:
                for it in prev[2 * (s - 1):2 * s]:
                    turn(it, 7)

    def finish(its):
        for it in its:
            add("acc", it=it)
        for it in its[0:2]:
            add("tick", it=it)
        gate()
        for it in its[2:4]:
            add("tick", it=it)
        for it in its[0:2]:
            turn(it, 4)
        add("tick", it=its[4])
        add("flush")
        gate()
        for it in its[2:]:
            turn(it, 4)

    def attention(br, heads, fill):
        seq = [(h, q) for h in heads for q in (*range(1, NT), 0)]
        ns, lag = (2, 1) if br == "A" else (1, 2)
        start = count["score"]
        count["score"] += ns * len(seq)
        parts, values = [], []

        def turn_probs(i):
            if i >= 0:
                h, q = seq[i]
                add("turnp", br=br, q=q, n=start + i * ns, first=i == 0)
                if q == 0:
                    values.append(h)

        for i in range(len(seq) + lag):
            if 1 <= i <= len(seq):
                add("soft", br=br, q=seq[i - 1][1], n=start + (i - 1) * ns)
            if lag == 2:
                turn_probs(i - lag)
            if i < len(seq):
                for m in range(ns):
                    add("score", br=br, h=seq[i][0], q=seq[i][1], m=m, n=start + i * ns + m, first=i == m == 0)
            with_values = bool(values)
            if values:
                add("values", br=br, h=values.pop())
                if lag == 1:
                    turn_probs(i - lag)
            if 0 <= i - lag + 1 < len(seq):
                h, q = seq[i - lag + 1]
                if q == 1:
                    prefetch(1)
                    parts = fill[h]()
                elif parts:
                    parts.pop(0)()
            if lag == 1 and not with_values:
                turn_probs(i - lag)
        if values:
            add("values", br=br, h=values.pop())

    def branch(b):
        add("osplit")
        for k in range(KD // 2):
            if k == 2:
                gate()
                gate()
            gemm("branch", b=b, k=k)
            add("merge", b=b, k=k)

    def queue_branch(b):
        queue("branch", [SUB] * 2, b=b, u=0, cols=(4, 2 * P))
        queue_gates(b, 6, 1)
        queue("branch", [SUB] * 2, b=b, u=1, cols=(4, 2 * P))

    add("first_ada")
    queue_ada(ADA_FIRST // 2)
    for c in (AQ, AK, AV):
        queue_tm(c, 512)
    queue_gates(0, 0, 2)
    queue_ada(1)
    queue_gates(0, 4, 1)
    queue_ada(1)
    queue_branch(0)
    add("norm", which=0)
    add("params")
    ada(3)
    add("spread")
    ada(ADA_FIRST // 2 - 3)
    ada_turn()
    add("mod", part=0)
    add("apply", which=0)

    aq = [item("aq", 512, [(0, 8, HD)], [G_DQ], "h" if t else None, t) for t in range(NT)]
    ak = [item("ak", 512, [(0, 8, HD)], [G_DK], "h" if t else None, t) for t in range(NT)]
    add("cache", b=0)
    chunk(512, True, [])
    chunk(512, False, aq)
    turn_cache(0)
    chunk(512, False, ak)
    for t in range(NT):
        add("acc", it=item("av", 512, [], [], None, t))
    attention("A", range(NH), {h: gate_parts for h in range(NH)})
    add("osq", h=0)
    for h in range(NH):
        if h + 1 < NH:
            add("osq", h=h + 1)
        add("ostat", h=h)
        (gate if h in (1, 2) else ada)()
        add("obcast", h=h)
        if h + 1 < NH:
            prefetch(2)
    queue_tm(BQ, BW)
    queue_gates(1, 0, 1)
    branch(0)

    cached = item("bc", BW, [(QR, 1, KVR)], [G_BKV], None, 1)
    bq = [item("bq", BW, [(0, 1, QR), (QR, 1, KVR)], [G_BQ, G_BKV], None, t) for t in range(NT)]
    add("cache", b=1)
    add("acc", it=cached)
    add("tick", it=cached)
    add("flush")
    for s in range(4):
        gemm("tm", w=BW, s=s, first=True, after_norm=False)
        if s == 0:
            at["turned"] = 4
            turn(cached, 4)
    finish(bq)
    for half in range(2):
        slot = count["unit"] % 2
        add("unit", src="mla", slot=slot, half=half, a=0)
        count["unit"] += 1
        at["held"] = slot
        queue_gates(1, 2 + 2 * half, 1)
        queue_ada(5)
        prefetch(1)
        its = [item("up", 4 * QK, [(0, 4, QK)], [G_MQ], "r" if t else None, t, q=True) for t in range(NT)]
        its += [item("up", 4 * QK, [(0, 4, QK)], [G_MK], "r" if t > 1 else None, t, q=False) for t in range(NK)]
        for i, it in enumerate(its):
            it["last"] = i == len(its) - 1
            it["slot_raw"] = slot
            it["bank"] = i % 4
            add("upmm", it=it, i=i, half=half)
            add("acc", it=it)
            add("tick", it=it)
            if it["last"]:
                at["held"] = None
            if i in (2, 6):
                gate()
            if i >= 3:
                turn(its[i - 3], 4)
            if i == 8:
                prefetch(2)
        add("flush")
        turn(its[-3], 4)
        ada()
        turn(its[-2], 4)
        turn(its[-1], 4)
        if half:
            queue_branch(1)
            for c, w in ((CK, 256), (CQ, 512)):
                queue_tm(c, w)
            queue_gates(2, 0, 1)
            for u in (2, 4):
                queue_ada(1)
                queue_gates(2, u, 1)
            queue_ada(2)
            queue_branch(2)
        attention("B", range(4 * half, 4 * half + 4), {h: ada_parts for h in range(4 * half, 4 * half + 4)})
    branch(1)

    ck = [item("ck", 256, [(0, 2, HD)], [G_GK], "h" if t else None, t) for t in range(NT)]
    cq = [item("cq", 512, [(0, 8, HD)], [G_GQ], "h" if t else None, t) for t in range(NT)]
    add("cache", b=2)
    turn_cache(2)
    chunk(256, True, [])
    chunk(512, False, ck)
    finish(cq)
    attention("C", range(GH), {h: gate_parts if h in (1, 2, 4, 5) else ada_parts for h in range(GH)})
    ada_turn()
    assert 2 * count["ada"] == 6 * KD
    add("mod", part=1)
    branch(2)

    def fm_units(kind, n, width, before, between=(), lag=0, **k):
        assert not pending and count["gemm"] == count["split"]
        count["unit"] += count["unit"] % 2

        def unit(s, a, **first):
            out = [dict(step="unit", src=kind, slot=s, a=a, **k)]
            for j in range(2):
                out.append(dict(step="split", slot=s, sub=j, off=j * width, width=width, last=j == 1,
                                cols=(KD, P) if kind == "wo" else None))
                out.append(dict(step=kind, sub=j, s=s, a=a, first=bool(first), **first, **k))
            return out

        def over(s, a, unit_before):
            u = unit(s, a)
            out = [dict(step=kind + "_out", s=1 - s, a=unit_before, **k)]
            out2 = [dict(step=kind + "_out2", s=1 - s, a=unit_before, **k)]
            return u[:2] + out + u[2:4] + out2 + u[4:]

        u = unit(0, 0, lag=lag)
        plan.extend(u[:2] + before[:1] + u[3:4] + before[1:] + list(between) + [u[2], u[4]])
        add("loop", n=n // 2 - 1, body=over(1, 1, 0) + over(0, 2, 1))
        plan.extend(over(1, n - 1, n - 2))
        count["unit"] += n
        return [dict(step=kind + "_out", s=1, a=n - 1, **k), dict(step=kind + "_out2", s=1, a=n - 1, **k)]

    add("zero", what="wo")
    left = fm_units("wo", KD // 2, SUB, [], [dict(step="msplit")])
    norm2 = [dict(step=x, which=1) for x in ("norm", "spread", "apply")]
    for f0, nf in FPARTS:
        left = fm_units("up", nf, SUB, left, () if f0 else norm2, lag=1 if f0 else 2, f0=f0, nf=nf)
        if f0:
            add("zero", what="down")
        left = fm_units("down", KD, nf // 2 * P, left, lag=2, f0=f0, nf=nf, squares=f0 > 0)
    plan.extend(left)
    assert count["gate"] == 3 * KD
    look_back(plan)
    return plan


def look_back(plan):
    splits, gemms, accs, ticks, softs, held = 0, 0, [], [], [], None
    sums = []
    used = {1: -2, 0: 0}
    for s in plan:
        k = s["step"]
        if k == "loop":
            look_back(s["body"])
            used = {1: splits - 2, 0: splits}
        elif k == "unit":
            s["lo_back"] = splits - used[s["slot"]]
            s["after_mla"] = held == s["slot"]
            held = s["slot"] if s["src"] == "mla" else None if s["after_mla"] else held
        elif k == "split":
            s["ahead"] = splits - gemms
            splits += 1
            used[s["slot"]] = splits
        elif k in ("ada", "tm", "gate", "branch", "wo", "up", "down"):
            gemms += 1
            s["lo_back"] = splits - gemms
        elif k == "gate_part":
            s["lo_back"] = splits - gemms - 1
        elif k == "acc":
            accs.append(id(s["it"]))
        elif k == "tick":
            s["acc_back"] = len(accs) - 1 - accs.index(id(s["it"]))
            s["sums_before"] = sums[-1] if sums else 0
            sums.append(len(s["it"]["groups"]))
            ticks.append(id(s["it"]))
        elif k == "turn":
            s["item_back"] = len(ticks) - 1 - ticks.index(id(s["it"]))
        elif k == "soft":
            softs.append(s["n"])
        elif k == "turnp":
            s["p_back"] = len(softs) - 1 - softs.index(s["n"])


def signals(s):
    k = s["step"]
    it = s.get("it")
    if k == "params":
        return dict(rows_loaded=16 * 7, gains_loaded=16 * 7, rows_turned=1, par_ready=1, gain_ready=3, lam_step=5, lam_exp=1)
    if k == "unit":
        return {f"raw_full{s['slot']}": 32 if s["src"] in ("mla", "up") else 16}
    if k == "first_ada":
        return {f"ada_full{u}": 16 for u in range(ADA_FIRST // 2)}
    if k == "ada_row":
        return dict(pair3_read=1)
    if k == "ada_turn":
        return dict(ada_done=1)
    if k == "mod":
        return dict(mod_ready=2)
    if k == "norm":
        return dict(stat_done=1, sums_read=1, nrs_ready=1, diag_ready=NT)
    if k == "spread":
        return dict(bc_done=1)
    if k == "apply":
        return dict(xn_done=KD, hf_ready=KD, hhi_ready=KD, hlo_ready=KD)
    if k == "split":
        return dict(hi_ready=1, lo_ready=1)
    if k == "tm":
        return dict(sub_done=1, acc_done=NT - 1 if s["s"] == 3 else 0)
    if k in ("ada", "gate", "branch", "wo", "up", "down"):
        return dict(sub_done=1, **(dict(pair3_read=1) if k == "gate" else {}))
    if k == "cache":
        return dict(cache_loaded=32)
    if k == "turnc":
        return dict(t_done=1, t_copied=1)
    if k == "acc":
        out = dict(acc_copied=1)
        if it["tile"] == 0:
            out["ctx_out"] = {"av": 16, "ck": 16, "bq": 32}.get(it["kind"], 0)
        return out
    if k == "tick":
        out = dict(sqr_done=1, ss_ready=len(it["groups"]), ms_done=len(it["groups"]), rstd_ready=1, xh_ready=1)
        if it["rope"]:
            out.update(gained=1, sin_ready=1, cos_done=1)
        return dict(out, item_ready=1)
    if k == "turn":
        out = dict(t_done=1, t_copied=1)
        if it["tile"] == 0:
            out["ctx_out"] = {"ak": 16, "ck": 16}.get(it["kind"], 0)
        return out
    if k == "upmm":
        return dict(up_done=1)
    if k == "score":
        return dict(score_done=1, max_ready=1, exp_done=1)
    if k == "soft":
        return dict(rden_done=1, p_ready=1, p1_done=1 if s["br"] == "A" else 0)
    if k == "turnp":
        return dict(pt_done=1, pt_copied=1)
    if k == "values":
        return dict(av_done=1, pair3_read=1)
    if k == "osq":
        return dict(osq_ready=1)
    if k == "ostat":
        return dict(ostat_done=1, sums_read=1, ors_ready=1, odiag_ready=NT)
    if k == "obcast":
        return dict(obc_done=1, pair3_read=1)
    if k == "osplit":
        return dict(ohi_ready=4, olo_ready=4)
    if k == "merge":
        return dict(fm_read=2, mg_ready=2 if s["b"] else 0)
    if k == "msplit":
        return dict(mhi_ready=KD, mlo_ready=KD)
    if k == "zero":
        return dict(zeroed=1)
    if k == "wo_out":
        return dict(fm_read=2, sq_ready=2)
    if k == "down_out":
        return dict(fm_read=1, sq_ready=int(s["squares"]))
    if k == "wo_out2":
        return dict(sq_added=2)
    if k == "down_out2":
        return dict(sq_added=int(s["squares"]))
    if k == "up_out":
        return dict(v_ready=2, tap_done=2, fm_read=2)
    if k == "up_out2":
        return dict(silu_done=1, prod_ready=1, ahi_ready=1, alo_ready=1)
    return {}


def total(plan):
    out = {}
    for s in plan:
        for name, n in (total(s["body"]) if s["step"] == "loop" else signals(s)).items():
            out[name] = out.get(name, 0) + n * (s["n"] if s["step"] == "loop" else 1)
    return out


CREDIT = 4
PLAN = build_plan()
PER_LAYER = total(PLAN)


class Count:

    def __init__(self, layer):
        self.layer, self.n, self.turn, self.per_turn = layer, {}, 0, {}

    def __call__(self, name, more=0):
        v = self.n.get(name, 0) + more + (0 if name in DMA_SEMS else CREDIT)
        v = self.layer * PER_LAYER[name] + v
        if self.per_turn.get(name, 0):
            v = v + self.turn * self.per_turn[name]
        return v

    def past(self, s, times=1):
        for name, n in (total(s["body"]) if s["step"] == "loop" else signals(s)).items():
            self.n[name] = self.n.get(name, 0) + n * times


DMA_SEMS = {"rows_loaded", "gains_loaded", "raw_full0", "raw_full1", "cache_loaded", "ctx_out",
            *(f"ada_full{u}" for u in range(ADA_FIRST // 2))}


def walk(eng, plan, wanted, emit, count):
    for s in plan:
        if s["step"] == "loop":
            if any(x["step"] in wanted for x in s["body"]):
                with eng.Fori(0, s["n"]) as turn:
                    count.turn, count.per_turn = turn, total(s["body"])
                    before = dict(count.n)
                    for x in s["body"]:
                        if x["step"] in wanted:
                            emit(x)
                        count.past(x)
                    count.n, count.turn, count.per_turn = before, 0, {}
            count.past(s, s["n"])
        else:
            if s["step"] in wanted:
                emit(s)
            count.past(s)


def turn_parts(it):
    return {"aq": [(i * P, P) for i in range(4)], "ak": [(i * P, P) for i in range(4)],
            "cq": [(i * P, P) for i in range(4)], "ck": [(0, P)], "bq": [(0, P), (P, P), (QR, P)], "bc": [(QR, P)],
            "up": [(i * QK, QK) for i in range(4)]}[it["kind"]]


def key_tile(it):
    return it["tile"] if it["kind"] in ("up", "bc") or not it["tile"] else it["tile"] + 1


def latent_tile(it):
    return it["tile"] - (2 if it["kind"] == "up" and not it["q"] else 1)


def span(it):
    a = it["groups"][0][0]
    b = it["groups"][-1]
    return a, b[0] + b[1] * b[2]


def program(nc, x_ctx, x_lat, c_lat, cache_dk, cache_dv, cache_ckv, cache_kpe, cache_gk, cache_gv, c_ctx,
            w_ada, b_ada, norm_mix, w_in, diff_qk_norm, diff_lambda, diff_out_norm, mla_q_norm, w_mla_q_up,
            mla_kv_norm, w_mla_kv_up, mla_qk_norm, gqa_qk_norm, w_a, w_b, w_c, w_o, norm_ffn, w_up, conv_w,
            conv_b, w_down, const_ident, const_rope_h, const_rope_r, const_layer,
            y_ctx, y_lat, new_dk, new_dv, new_ckv, new_kpe, new_gk, new_gv):
    ctx = ExitStack()
    with ctx:
        def sb(name, shape, dt=F32):
            return ctx.enter_context(nc.sbuf_tensor(name, shape, dt))

        def over(*groups):
            out, most = [], 0
            for g in groups:
                with ExitStack() as st:
                    size = 0
                    for name, shape, dt in g:
                        out.append(st.enter_context(nc.sbuf_tensor(name, shape, dt)))
                        size += int(np.prod(shape[1:])) * 4
                    most = max(most, size)
            sb("room_" + groups[0][0][0], [P, most // 4])
            return out

        ident, ones = sb("ident", [P, P]), sb("ones", [P, P])
        xT = sb("xT", [P, KD, T])
        hhi, hlo = sb("hhi", [P, KD, T], F32R), sb("hlo", [P, KD, T], F32R)
        raw = sb("raw", [P, 2, 2 * SUB])
        whi, wlo = sb("whi", [P, 2, SUB], F32R), sb("wlo", [P, 2, SUB], F32R)
        rows = sb("rows", [P, 3, P])
        ada_rows = rows[0:4, 0:2, :].rearrange("p a b -> p (a b)")
        PT = sb("PT", [P, NPAR])
        gains = sb("gains", [P, NGAIN])
        lamv = sb("lamv", [P, 4, HD])
        lam2, lame, neglam, dgain = sb("lam2", [P, 2]), sb("lame", [P, 2]), sb("neglam", [P, 1]), sb("dgain", [P, 1])
        mod = sb("mod", [P, 6 * KD, 2])
        scale = sb("scale", [P, 2, KD, 2])
        cT = sb("cT", [P, KD, 2])
        csplit = sb("csplit", [P, KD, 4], F32R)
        add2 = sb("add2", [4, 2])
        crow = sb("crow", [2 * KD, P])
        ropeh, roper = sb("ropeh", [P, NT - 1, 2, HD]), sb("roper", [P, NT - 1, 2, ROPE])
        ckv_out = sb("ckv_out", [P, KVR + ROPE])
        epsc, mhalf = sb("epsc", [P, 1]), sb("mhalf", [P, 8])
        ssum, smean, rstd = sb("ssum", [P, 2, 8]), sb("smean", [P, 2, 8]), sb("rstd", [P, 2, 8])
        negmax, den, rden = sb("negmax", [P, 4]), sb("den", [P, 4]), sb("rden", [P, 4])
        nmean, nrstd = sb("nmean", [P, NT]), sb("nrstd", [P, NT])

        (stage, tmpq, tmpc, tmps, prob, probT, probTc, ohi, olo, nsq, hf, diag, xin) = over(
            [("stage", [P, 5, 512], F32), ("tmpq", [P, 2, 512], F32), ("tmpc", [P, 512], F32), ("tmps", [P, 512], F32)],
            [("prob", [P, 4, T], F32), ("probT", [P, NT, DEC], F32), ("probTc", [P, P], F32)],
            [("ohi", [P, 4, T], F32R), ("olo", [P, 4, T], F32R)],
            [("nsq", [P, 2, T], F32), ("hf", [P, 4, T], F32), ("diag", [P, NT, P], F32)],
            [("xin", [P, NT, D], F32)])
        mixers = [("merged", [P, KD, T], F32), ("gated", [P, GATE_SLOTS, T], F32), ("oT", [P, 4, T], F32)]
        branches = [[("qA", [P, 4, T], F32), ("kA", [P, 4, KEYS], F32), ("vA", [P, NK, 512], F32)],
                    [("bqT", [P, 2, T], F32), ("ckvT", [P, KEYS], F32), ("kpe", [P, NK, ROPE], F32),
                     ("qB", [P, 4, T], F32), ("kB", [P, 4, KEYS], F32), ("vB", [P, NK, 4, 64], F32)],
                    [("qC", [P, 4, T], F32), ("kC", [P, KEYS], F32), ("vC", [P, NK, 128], F32)]]
        ffn = [("ahi", [P, 12, T], F32R), ("alo", [P, 12, T], F32R), ("va", [P, 2, T], F32), ("vg", [P, 2, T], F32)]
        with ExitStack() as st:
            merged, gated, oT = [st.enter_context(nc.sbuf_tensor(*x)) for x in mixers]
            made = []
            for g in branches:
                with ExitStack() as st2:
                    made += [st2.enter_context(nc.sbuf_tensor(*x)) for x in g]
        (qA, kA, vA, bqT, ckvT, kpe, qB, kB, vB, qC, kC, vC) = made
        size = max(sum(int(np.prod(x[1][1:])) for x in mixers + g) for g in branches)
        (ahi, alo, va, vg, adaw, room) = over(ffn, [("adaw", [P, ADA_FIRST // 2, 2 * SUB], F32)], [("mixroom", [P, size], F32)])
        cached = oT[:, :, :].rearrange("p a b -> p (a b)")
        ps = ctx.enter_context(nc.psum_tensor("ps", [P, 8 * 512], F32))

        first_squares = [nsq[:, 0, :], nsq[:, 1, :], hf[:, 1, :], hf[:, 2, :], hf[:, 3, :]]

        def bank(b, n=512, p0=0, p1=P):
            return ps[p0:p1, b * 512:b * 512 + n]

        def run(pair, lo=0, hi=T, p0=0, p1=P):
            return ps[p0:p1, pair * 1024 + OFF + lo:pair * 1024 + OFF + hi]

        def halves(pair):
            return [(run(pair, 0, HALF), 0), (run(pair, HALF, T), HALF)]

        def line(pair, n=T, p0=0, p1=P, off=0):
            return ps[p0:p1, pair * 1024 + off:pair * 1024 + off + n]

        def sub_views(s):
            slot, w, sub = s["slot"], s["width"], s["sub"]
            if slot >= 2:
                return adaw[:, slot - 2, s["off"]:s["off"] + w], lambda x: x[:, sub, 0:w]
            if s["cols"]:
                k, c = s["cols"]
                j = 1 if s["last"] else 0
                src = raw[:, slot, :].rearrange("p (k c) -> p k c", k=k)[:, :, j * c:(j + 1) * c]
                return src, lambda x: x[:, sub, :].rearrange("p (k c) -> p k c", k=k)
            return raw[:, slot, s["off"]:s["off"] + w], lambda x: x[:, sub, 0:w]

        def rope_views(it):
            c, nh, dh = it["groups"][0]
            r0, half = (0, HD // 2) if it["rope"] == "h" else (NOPE, ROPE // 2)
            table = ropeh if it["rope"] == "h" else roper
            w = 2 * half
            x = stage[:, it["slot"], 0:nh * dh].rearrange("p (h d) -> p h d", h=nh)[:, :, r0:r0 + w]
            cs = [table[:, latent_tile(it), j, :].unsqueeze(1).to_broadcast([P, nh, w]) for j in range(2)]
            tc, ts = [x_[:, 0:nh * w].rearrange("p (h d) -> p h d", h=nh) for x_ in (tmpc, tmps)]
            return r0, half, x, cs, tc, ts

        sems = {n: ctx.enter_context(nc.semaphore(n)) for n in list(PER_LAYER) +
                ["ident_loaded", "const_loaded", "const_set", "x_loaded", "x_turned", "x_copied", "x_squared", "x_summed",
                 "c_turned", "c_ready",
                 "y_turned", "y_copied", "y_out"]}
        S = sems
        block = ctx.enter_context(nc.Block())

        @block.sync
        def _(sp):
            sp.dma_start(ident[:, :], const_ident).then_inc(S["ident_loaded"], 16)
            sp.dma_start(xin[:, 0, :], x_ctx[0]).then_inc(S["x_loaded"], 16)
            sp.dma_start(xin[:, 1:NT, :], x_lat[0].rearrange("(t p) d -> p t d", p=P)).then_inc(S["x_loaded"], 16)
            for j in range(2):
                sp.dma_start(add2[2 * j:2 * j + 2, :], const_ident[0:2, 0:2]).then_inc(S["const_loaded"], 16)
            sp.dma_start(crow[0:KD, :], c_ctx.rearrange("(k p) -> k p", p=P)).then_inc(S["const_loaded"], 16)
            sp.dma_start(crow[KD:2 * KD, :], c_lat.rearrange("a (k p) -> (a k) p", p=P)).then_inc(S["const_loaded"], 16)
            sp.dma_start(ropeh[:, :, :, :], const_rope_h).then_inc(S["const_loaded"], 16)
            sp.dma_start(roper[:, :, :, :], const_rope_r).then_inc(S["const_loaded"], 16)
            with sp.Fori(0, DEPTH) as layer:
                n = Count(layer)

                def at(x):
                    return x[ds(layer, 1)]

                def row(x, a, b):
                    return at(x)[:, a:b]

                def load_params():
                    sp.wait_ge(S["par_ready"], n("par_ready"))
                    sp.wait_ge(S["hlo_ready"], n("hlo_ready"))
                    for at_row, x, k in ((P_ADA, b_ada, 48), (P_NM, norm_mix, KD), (P_NF, norm_ffn, KD), (P_CB, conv_b, 44),
                                         (P_DN, diff_out_norm, 1)):
                        sp.dma_start(rows[at_row:at_row + k, 0, :], at(x).rearrange("l (k p) -> (l k) p", p=P))\
                          .then_inc(S["rows_loaded"], 16)
                    sp.dma_start(rows[0:88, 1, :], at(conv_w)[:, 0:2, :].rearrange("l w (k p) -> (l w k) p", p=P))\
                      .then_inc(S["rows_loaded"], 16)
                    sp.dma_start(rows[0:44, 2, :], at(conv_w)[:, 2:3, :].rearrange("l w (k p) -> (l w k) p", p=P))\
                      .then_inc(S["rows_loaded"], 16)
                    for g, x, k in ((G_DQ, at(diff_qk_norm).rearrange("l a b -> l (a b)"), 2 * HD),
                                    (G_GQ, at(gqa_qk_norm).rearrange("l a b -> l (a b)"), 2 * HD),
                                    (G_MQ, at(mla_qk_norm).rearrange("l a b -> l (a b)"), 2 * QK),
                                    (G_BQ, at(mla_q_norm), QR), (G_BKV, at(mla_kv_norm), KVR),
                                    (G_LC, at(const_layer), 2)):
                        sp.dma_start(gains[:, g:g + k], x.to_broadcast([P, k])).then_inc(S["gains_loaded"], 16)
                    sp.dma_start(lamv[:, :, :].rearrange("p a b -> p (a b)"),
                                 at(diff_lambda).rearrange("l a b -> l (a b)").to_broadcast([P, 4 * HD]))\
                      .then_inc(S["gains_loaded"], 16)

                def load_first_ada(s):
                    used = n("sub_done")
                    sp.wait_ge(S["sub_done"], used)
                    for u in range(ADA_FIRST // 2):
                        if u == ADA_EARLY:
                            load_params()
                        sp.dma_start(adaw[:, u, :].rearrange("p (k c) -> p k c", k=KD), at(w_ada)[:, :, u * 256:(u + 1) * 256]
                                     .rearrange("l (k p) c -> p (l k) c", p=P)).then_inc(S[f"ada_full{u}"], 16)

                def load_unit(s):
                    src, slot = s["src"], s["slot"]
                    full = S[f"raw_full{slot}"]
                    r = raw[:, slot, :]
                    if s.get("after_mla"):
                        sp.wait_ge(S["up_done"], n("up_done"))
                    else:
                        sp.wait_ge(S["lo_ready"], n("lo_ready", -s["lo_back"]))
                    u = n.turn * 2 + s["a"]
                    if src == "ada":
                        sp.dma_start(r.rearrange("p (k c) -> p k c", k=KD),
                                     at(w_ada)[:, :, s["u"] * 256:(s["u"] + 1) * 256]
                                     .rearrange("l (k p) c -> p (l k) c", p=P)).then_inc(full, 16)
                    elif src == "tm":
                        w = s["w"]
                        sp.dma_start(r[:, 0:4 * w].rearrange("p (k c) -> p k c", k=4),
                                     at(w_in)[:, s["u"] * 512:(s["u"] + 1) * 512, s["col"]:s["col"] + w]
                                     .rearrange("l (k p) c -> p (l k) c", p=P)).then_inc(full, 16)
                    elif src == "gate":
                        sp.dma_start(r.rearrange("p (k c) -> p k c", k=KD), at(w_in)[:, :, s["col"]:s["col"] + 256]
                                     .rearrange("l (k p) c -> p (l k) c", p=P)).then_inc(full, 16)
                    elif src == "branch":
                        w = (w_a, w_b, w_c)[s["b"]]
                        sp.dma_start(r.rearrange("p (k c) -> p k c", k=4),
                                     at(w)[:, :, s["u"] * 512:(s["u"] + 1) * 512]
                                     .rearrange("l (k p) c -> p (l k) c", p=P)).then_inc(full, 16)
                    elif src == "mla":
                        h = s["half"]
                        sp.dma_start(r[:, 0:768].rearrange("p (k c) -> p k c", k=2),
                                     at(w_mla_q_up)[:, :, h * 384:(h + 1) * 384].rearrange("l (k p) c -> p (l k) c", p=P))\
                          .then_inc(full, 16)
                        sp.dma_start(r[:, 768:1280], at(w_mla_kv_up)[:, :, h * 512:(h + 1) * 512]
                                     .rearrange("l p c -> p (l c)")).then_inc(full, 16)
                    elif src == "wo":
                        sp.dma_start(r.rearrange("p (k c) -> p k c", k=KD), at(w_o)[:, :, ds(u * 256, 256)]
                                     .rearrange("l (k p) c -> p (l k) c", p=P)).then_inc(full, 16)
                    elif src == "up":
                        for j in range(2):
                            sp.dma_start(r[:, j * SUB:(j + 1) * SUB].rearrange("p (k c) -> p k c", k=KD),
                                         at(w_up)[:, :, ds((u + s["f0"]) * P + j * FF, P)]
                                         .rearrange("l (k p) c -> p (l k) c", p=P)).then_inc(full, 16)
                    elif src == "down":
                        nf, f0 = s["nf"], s["f0"]
                        sp.dma_start(r[:, 0:nf * P].rearrange("p (k c) -> p k c", k=nf),
                                     at(w_down)[:, f0 * P:(f0 + nf) * P, ds(u * P, P)]
                                     .rearrange("l (k p) c -> p (l k) c", p=P)).then_inc(full, 16)

                def emit(s):
                    if s["step"] == "first_ada":
                        load_first_ada(s)
                    else:
                        load_unit(s)

                walk(sp, PLAN, ("first_ada", "unit"), emit, n)
            for t in range(NT):
                sp.wait_ge(S["y_copied"], 2 * t + 2)
                sp.dma_start(y_ctx[0] if t == 0 else y_lat[0, (t - 1) * P:t * P, :], xin[:, t, :]).then_inc(S["y_out"], 16)
            sp.wait_ge(S["y_out"], 16 * NT)
            sp.wait_ge(S["ctx_out"], DEPTH * PER_LAYER["ctx_out"])

        @block.tensor
        def _(pe):
            pe.wait_ge(S["ident_loaded"], 16)
            pe.wait_ge(S["x_loaded"], 32)
            for t in range(NT):
                for j in range(2):
                    if t * 2 + j >= 4:
                        pe.wait_ge(S["x_copied"], t * 2 + j - 3)
                    for i in range(4):
                        f = j * 4 + i
                        mm = pe.transpose(bank((t * 2 + j) % 4)[:, i * P:(i + 1) * P], xin[:, t, f * P:(f + 1) * P], ident[:, :])
                    mm.then_inc(S["x_turned"], 1)
            pe.wait_ge(S["const_loaded"], 16 * 6)
            pe.wait_ge(S["const_set"], 4)
            pe.transpose(bank(7, 2 * KD), crow[:, :], ident[0:2 * KD, 0:2 * KD]).then_inc(S["c_turned"], 1)
            with pe.Fori(0, DEPTH) as layer:
                n = Count(layer)

                def params(s):
                    pe.wait_ge(S["rows_loaded"], n("rows_loaded", 112))
                    pe.wait_ge(S["fm_read"], n("fm_read"))
                    pe.transpose(bank(5)[:, 0:109], rows[0:109, 0, :], ident[0:109, 0:109])
                    pe.transpose(bank(5)[:, 109:197], rows[0:88, 1, :], ident[0:88, 0:88])
                    pe.transpose(bank(5)[:, 197:241], rows[0:44, 2, :], ident[0:44, 0:44]).then_inc(S["rows_turned"], 1)

                def pair3_free():
                    pe.wait_ge(S["pair3_read"], n("pair3_read"))
                    pe.wait_ge(S["sums_read"], n("sums_read"))
                    pe.wait_ge(S["mod_ready"], n("mod_ready"))
                    pe.wait_ge(S["t_copied"], n("t_copied"))

                def ada(s):
                    sub_waits(s)
                    pair3_free()
                    for i in range(4):
                        for w in (whi, wlo):
                            mm = pe.matmul(bank(6)[0:4, 256:512], csplit[:, 4 * s["j"] + i, :],
                                           w[:, s["sub"], i * 256:(i + 1) * 256],
                                           start=s["j"] == i == 0 and w is whi, stop=s["j"] == 1 and i == 3 and w is wlo)
                    mm.then_inc(S["sub_done"], 1)

                def ada_turn(s):
                    pair3_free()
                    u = s["u"]
                    for j in range(2):
                        c = ADA_AT + 2 * (2 * u + j - (0 if 2 * u < ADA_FIRST else ADA_FIRST))
                        mm = pe.matmul(bank(6)[:, c:c + 2], ada_rows[:, j * P:(j + 1) * P], add2[0:4, :],
                                       start=True, stop=True)
                    mm.then_inc(S["ada_done"], 1)

                def spread_rows(outs, diag_t, ready, signal):
                    pe.wait_ge(S[ready[0]], ready[1])
                    rhs = diag_t.rearrange("p t c -> p (t c)")
                    for out, c in outs:
                        mm = pe.matmul(out, ones[:, :], rhs[:, c:c + HALF], start=True, stop=True)
                    mm.then_inc(S[signal], 1)

                def norm(s):
                    pe.wait_ge(S["c_ready"], 3)
                    pe.wait_ge(S["x_summed"], KD - 1)
                    pe.wait_ge(S["sq_added"], n("sq_added"))
                    for t in range(NT):
                        mm = pe.matmul(bank(6)[:, t:t + 1], hf[:, 0, t * P:(t + 1) * P], ones[:, 0:1], start=True, stop=True)
                    mm.then_inc(S["stat_done"], 1)

                def spread(s):
                    pe.wait_ge(S["par_ready"], n("par_ready"))
                    pe.wait_ge(S["pair3_read"], n("pair3_read"))
                    spread_rows([(bank(5, HALF), 0), (bank(7, HALF), HALF)], diag[:, :, :], ("diag_ready", n("diag_ready")), "bc_done")

                def sub_waits(s):
                    pe.wait_ge(S["lo_ready"], n("lo_ready", -s["lo_back"]))

                def tm(s):
                    sub, w = s["sub"], s["w"]
                    sub_waits(s)
                    pe.wait_ge(S["hlo_ready"], n("hlo_ready", 2 * s["s"] + 2 - KD if s["after_norm"] else 0))
                    for t in range(NT):
                        if s["s"] == 0:
                            if s["first"]:
                                pe.wait_ge(S["fm_read"], n("fm_read"))
                            else:
                                pe.wait_ge(S["acc_copied"], n("acc_copied", t + 1 - NT))
                        for k in range(2):
                            kt = 2 * s["s"] + k
                            c = slice(t * P, (t + 1) * P)
                            wh, wl = whi[:, sub, k * w:(k + 1) * w], wlo[:, sub, k * w:(k + 1) * w]
                            out = bank(t, w)
                            pe.matmul(out, hhi[:, kt, c], wh, start=kt == 0, stop=False)
                            pe.matmul(out, hhi[:, kt, c], wl, start=False, stop=False)
                            mm = pe.matmul(out, hlo[:, kt, c], wh, start=False, stop=kt == KD - 1)
                        if s["s"] == 3 and t < NT - 1:
                            mm.then_inc(S["acc_done"], 1)
                    mm.then_inc(S["sub_done"], 1)

                def feature_tile(pair, sub, ks, step, off, mh, ml, first=True, last=True, base=0, made=None):
                    for i, kt in enumerate(ks):
                        if made:
                            pe.wait_ge(S[made], n(made, i + 1 - len(ks)))
                        c = slice((kt - base) * step + off, (kt - base) * step + off + P)
                        for w, m, a in ((whi, mh, 0), (whi, ml, 1), (wlo, mh, 2)):
                            for out, o in halves(pair):
                                mm = pe.matmul(out, w[:, sub, c], m[:, kt, o:o + HALF],
                                               start=first and i == 0 and a == 0, stop=last and i == len(ks) - 1 and a == 2)
                    return mm

                def gate_part(s):
                    ks = s["ks"]
                    if ks[0] == 0:
                        sub_waits(s)
                        pair3_free()
                    return feature_tile(3, s["sub"], ks, P, 0, hhi, hlo, first=ks[0] == 0, last=ks[-1] == KD - 1)

                def gate(s):
                    gate_part(s).then_inc(S["sub_done"], 1)

                def branch(s):
                    sub_waits(s)
                    if s["k"] == 0:
                        pe.wait_ge(S["exp_done"], n("exp_done"))
                        pe.wait_ge(S["pt_copied"], n("pt_copied"))
                    for j in range(2):
                        i = 2 * s["k"] + j
                        if i >= 3:
                            pe.wait_ge(S["fm_read"], n("fm_read", j - 2))
                        mm = feature_tile(i % 3, s["sub"], range(4), 2 * P, j * P, ohi, olo,
                                          made="olo_ready" if i == 0 else None)
                    mm.then_inc(S["sub_done"], 1)

                def fm_waits(s, lag):
                    pe.wait_ge(S["fm_read"], n("fm_read", -(s["lag"] if s["first"] else lag)))

                def wo(s):
                    sub_waits(s)
                    if s["first"]:
                        pe.wait_ge(S["pair3_read"], n("pair3_read"))
                    fm_waits(s, 2)
                    feature_tile(2 * s["s"] + s["sub"], s["sub"], range(KD), P, 0, hhi, hlo,
                                 made="mlo_ready" if s["first"] and s["sub"] == 0 else None).then_inc(S["sub_done"], 1)

                def up(s):
                    sub_waits(s)
                    fm_waits(s, 2)
                    feature_tile(2 * s["s"] + s["sub"], s["sub"], range(KD), P, 0, hhi, hlo,
                                 made="hlo_ready" if s["first"] and s["sub"] == 0 else None).then_inc(S["sub_done"], 1)

                def down(s):
                    sub_waits(s)
                    half = s["nf"] // 2
                    if s["first"] and s["sub"] == 0:
                        pe.wait_ge(S["alo_ready"], n("alo_ready", -half))
                    fm_waits(s, 1)
                    feature_tile(2 * s["s"], s["sub"], range(s["sub"] * half, (s["sub"] + 1) * half), P, 0, ahi, alo,
                                 first=s["sub"] == 0, last=s["sub"] == 1, base=s["sub"] * half,
                                 made="alo_ready" if s["first"] and s["sub"] else None).then_inc(S["sub_done"], 1)

                def turnc(s):
                    pe.wait_ge(S["cache_loaded"], n("cache_loaded"))
                    pe.wait_ge(S["fm_read"], n("fm_read"))
                    pe.wait_ge(S["t_copied"], n("t_copied"))
                    for i in range(4 if s["b"] == 0 else 1):
                        mm = pe.transpose(bank(5)[:, i * P:(i + 1) * P], cached[:, i * P:(i + 1) * P], ident[:, :])
                    mm.then_inc(S["t_done"], 1)

                def turn(s):
                    it = s["it"]
                    src = stage[:, it["slot"], :]
                    pe.wait_ge(S["item_ready"], n("item_ready", -s["item_back"]))
                    pe.wait_ge(S["t_copied"], n("t_copied", -1))
                    if s["bank"] == 5:
                        pe.wait_ge(S["pt_copied"], n("pt_copied"))
                    elif s["bank"] == 4:
                        pe.wait_ge(S["acc_copied"], n("acc_copied"))
                    else:
                        pe.wait_ge(S["pair3_read"], n("pair3_read"))
                    for i, (c, w) in enumerate(turn_parts(it)):
                        mm = pe.transpose(bank(s["bank"])[0:w, i * P:(i + 1) * P], src[:, c:c + w], ident[:, :])
                    mm.then_inc(S["t_done"], 1)

                def upmm(s):
                    it, i = s["it"], s["i"]
                    slot = it["slot_raw"]
                    if i == 0:
                        pe.wait_ge(S[f"raw_full{slot}"], n(f"raw_full{slot}"))
                        pe.wait_ge(S["t_copied"], n("t_copied"))
                        pe.wait_ge(S["exp_done"], n("exp_done"))
                        pe.wait_ge(S["acc_copied"], n("acc_copied"))
                    if i >= 4:
                        pe.wait_ge(S["acc_copied"], n("acc_copied", -3))
                    t = it["tile"]
                    if it["q"]:
                        for k in range(2):
                            mm = pe.matmul(bank(i % 4, 384), bqT[:, k, t * P:(t + 1) * P],
                                           raw[:, slot, k * 384:(k + 1) * 384], start=k == 0, stop=k == 1)
                    else:
                        mm = pe.matmul(bank(i % 4), ckvT[:, t * P:(t + 1) * P], raw[:, slot, 768:1280], start=True, stop=True)
                    mm.then_inc(S["up_done"], 1)

                def score(s):
                    h, q, br = s["h"], s["q"], s["br"]
                    pair = s["n"] % 2
                    if s["first"]:
                        pe.wait_ge(S["t_copied"], n("t_copied"))
                        pe.wait_ge(S["acc_copied"], n("acc_copied"))
                        pe.wait_ge(S["cache_loaded"], n("cache_loaded"))
                    pe.wait_ge(S["exp_done"], n("exp_done", -1))
                    if br == "A":
                        m = s["m"] * NH + h
                        tile, p0, kk = m // 2, m % 2 * HD, HD
                        qt, kt = qA[p0:p0 + kk, tile, :], kA[p0:p0 + kk, tile, :]
                    elif br == "B":
                        qt, kt = qB[0:QK, h % 4, :], kB[0:QK, h % 4, :]
                    else:
                        p0 = h // 4 * HD
                        qt, kt = qC[p0:p0 + HD, h % 4, :], kC[p0:p0 + HD, :]
                    qs = qt[:, q * P:(q + 1) * P]
                    if q == 0:
                        mm = pe.matmul(run(pair, 0, SEQ), qs, kt[:, 0:SEQ], start=True, stop=True)
                    else:
                        for out, c in halves(pair):
                            mm = pe.matmul(out, qs, kt[:, SEQ + c:SEQ + c + HALF], start=True, stop=True)
                    mm.then_inc(S["score_done"], 1)

                def turnp(s):
                    q, slot = s["q"], s["n"] % 4
                    if s["first"]:
                        pe.wait_ge(S["acc_copied"], n("acc_copied"))
                    pe.wait_ge(S["p_ready"], n("p_ready", -s["p_back"]))
                    pe.wait_ge(S["pt_copied"], n("pt_copied"))
                    for i in range(1 if q == 0 else NT):
                        mm = pe.transpose(line(2, P, off=i * P), prob[:, slot, i * P:(i + 1) * P], ident[:, :])
                    mm.then_inc(S["pt_done"], 1)

                def values(s):
                    h, br = s["h"], s["br"]
                    pe.wait_ge(S["pt_copied"], n("pt_copied"))
                    pe.wait_ge(S["pair3_read"], n("pair3_read"))
                    if br == "A":
                        p0, p1, v = 0, P, [vA[:, k, h * VD:(h + 1) * VD] for k in range(NK)]
                    elif br == "B":
                        p0, v = h % 2 * 64, [vB[:, k, h % 4, :] for k in range(NK)]
                    else:
                        p0, v = h % 2 * 64, [vC[:, k, h // 4 * 64:h // 4 * 64 + 64] for k in range(NK)]
                    p1 = p0 + (P if br == "A" else 64)
                    pe.matmul(line(3, SEQ, p0, p1, off=512 - SEQ), v[0], probTc[:, :], start=True, stop=True)
                    for k in range(NT):
                        mm = pe.matmul(line(3, DEC, p0, p1, off=512), v[k + 1], probT[:, k, :], start=k == 0, stop=k == NT - 1)
                    mm.then_inc(S["av_done"], 1)

                def ostat(s):
                    pe.wait_ge(S["osq_ready"], n("osq_ready", 0 if s["h"] == NH - 1 else -1))
                    pe.wait_ge(S["pair3_read"], n("pair3_read"))
                    for t in range(NT):
                        mm = pe.matmul(bank(6)[:, t:t + 1], nsq[:, s["h"] % 2, t * P:(t + 1) * P], ones[:, 0:1],
                                       start=t == 0, stop=True, skip_group_check=True)
                    mm.then_inc(S["ostat_done"], 1)

                def obcast(s):
                    pe.wait_ge(S["pair3_read"], n("pair3_read"))
                    spread_rows(halves(3), diag[:, :, :], ("odiag_ready", n("odiag_ready")), "obc_done")

                do = dict(params=params, ada=ada, ada_turn=ada_turn, norm=norm, spread=spread, tm=tm, gate_part=gate_part, gate=gate, branch=branch, wo=wo, up=up, down=down,
                          turnc=turnc, turn=turn, upmm=upmm, score=score, turnp=turnp, values=values, ostat=ostat,
                          obcast=obcast)
                walk(pe, PLAN, do, lambda s: do[s["step"]](s), n)
            for t in range(NT):
                for j in range(2):
                    if t == j == 0:
                        pe.wait_ge(S["fm_read"], DEPTH * PER_LAYER["fm_read"] + CREDIT)
                    if 2 * t + j >= 4:
                        pe.wait_ge(S["y_copied"], 2 * t + j - 3)
                    for i in range(4):
                        mm = pe.transpose(bank((2 * t + j) % 4)[:, i * P:(i + 1) * P],
                                          xT[:, 4 * j + i, t * P:(t + 1) * P], ident[:, :])
                    mm.then_inc(S["y_turned"], 1)

        @block.scalar
        def _(act):
            for t in range(NT):
                for j in range(2):
                    act.wait_ge(S["x_turned"], 2 * t + j + 1)
                    act.activation(xT[:, 4 * j:4 * j + 4, t * P:(t + 1) * P],
                                   bank((t * 2 + j) % 4).rearrange("p (i c) -> p i c", c=P), ACT.Copy).then_inc(S["x_copied"], 1)
            act.wait_ge(S["c_turned"], 1)
            act.activation(cT[:, :, :].rearrange("p k j -> p j k"), bank(7, 2 * KD).rearrange("p (j k) -> p j k", j=2),
                           ACT.Silu).then_inc(S["c_ready"], 1)
            act.wait_ge(S["c_ready"], 1)
            act.activation(csplit[:, :, 0:2], cT[:, :, :], ACT.Copy).then_inc(S["c_ready"], 1)
            act.wait_ge(S["x_copied"], 2 * NT)
            for k in range(KD):
                if k >= 5:
                    act.wait_ge(S["x_summed"], max(1, k - 5))
                act.activation(first_squares[k % 5], xT[:, k, :], ACT.Square).then_inc(S["x_squared"], 1)
            with act.Fori(0, DEPTH) as layer:
                n = Count(layer)

                def params(s):
                    act.wait_ge(S["rows_turned"], n("rows_turned", 1))
                    act.activation(PT[:, :], bank(5, NPAR), ACT.Copy).then_inc(S["par_ready"], 1)
                    act.wait_ge(S["lam_step"], n("lam_step", 3))
                    act.activation(lame[:, :], lam2[:, :], ACT.Exp).then_inc(S["lam_exp"], 1)

                def norm(s):
                    if s["which"]:
                        act.wait_ge(S["ctx_out"], n("ctx_out"))

                def squares(f, slot, j):
                    act.wait_ge(S["fm_read"], n("fm_read", j + 1))
                    act.wait_ge(S["sq_added"], n("sq_added"))
                    act.activation(nsq[:, slot:slot + 1, :], xT[:, ds(f, 1), :], ACT.Square).then_inc(S["sq_ready"], 1)

                def wo_out(s):
                    for j in range(2):
                        squares((n.turn * 2 + s["a"]) * 2 + j, j, j)

                def down_out(s):
                    if s["squares"]:
                        squares(n.turn * 2 + s["a"], s["s"], 0)

                def apply(s):
                    for k in range(KD):
                        act.wait_ge(S["hf_ready"], n("hf_ready", k + 1))
                        act.activation(hhi[:, k, :], hf[:, k % 4, :], ACT.Copy).then_inc(S["hhi_ready"], 1)

                def split(s):
                    slot, sub, w = s["slot"], s["sub"], s["width"]
                    if slot < 2:
                        act.wait_ge(S[f"raw_full{slot}"], n(f"raw_full{slot}"))
                    else:
                        act.wait_ge(S[f"ada_full{slot - 2}"], n(f"ada_full{slot - 2}"))
                    act.wait_ge(S["sub_done"], n("sub_done", s["ahead"] - 1))
                    src, dst = sub_views(s)
                    act.activation(dst(whi), src, ACT.Copy).then_inc(S["hi_ready"], 1)

                def acc(s):
                    it = s["it"]
                    kind, t = it["kind"], it["tile"]
                    kt = key_tile(it)
                    if n.n.get("ctx_out"):
                        act.wait_ge(S["ctx_out"], n("ctx_out"))
                    if kind == "bc":
                        act.wait_ge(S["cache_loaded"], n("cache_loaded"))
                        act.wait_ge(S["sub_done"], n("sub_done"))
                    elif kind == "up":
                        act.wait_ge(S["up_done"], n("up_done"))
                    elif t < NT - 1:
                        act.wait_ge(S["acc_done"], n("acc_done", t + 2 - NT))
                    else:
                        act.wait_ge(S["sub_done"], n("sub_done"))
                    if kind in ("aq", "ak", "av", "cq", "ck", "bq") and it["groups"] and t == 0:
                        act.wait_ge(S["hlo_ready"], n("hlo_ready"))
                    b = it["bank"]
                    st = stage[:, it["slot"], :] if it["groups"] else None
                    if kind in ("aq", "ak"):
                        act.activation(st, bank(b), ACT.Copy).then_inc(S["acc_copied"], 1)
                    elif kind == "cq":
                        act.activation(st.rearrange("p (r g d) -> p r g d", r=4, g=2),
                                       bank(b).rearrange("p (g r d) -> p r g d", r=4, g=2), ACT.Copy).then_inc(S["acc_copied"], 1)
                    elif kind == "av":
                        act.activation(vA[:, kt, :], bank(b), ACT.Copy).then_inc(S["acc_copied"], 1)
                        if t == 0:
                            act.wait_ge(S["acc_copied"], n("acc_copied", 1))
                            act.dma_start(new_dv[0, ds(layer, 1)].rearrange("l p h d -> p (l h d)"), vA[:, 0, :])\
                               .then_inc(S["ctx_out"], 16)
                    elif kind == "ck":
                        act.activation(st[:, 0:P], bank(b)[:, 0:P], ACT.Copy)
                        act.activation(vC[:, kt, :], bank(b)[:, P:2 * P], ACT.Copy).then_inc(S["acc_copied"], 1)
                        if t == 0:
                            act.wait_ge(S["acc_copied"], n("acc_copied", 1))
                            act.dma_start(new_gv[0, ds(layer, 1)].rearrange("l p h d -> p (l h d)"), vC[:, 0, :])\
                               .then_inc(S["ctx_out"], 16)
                    elif kind == "bq":
                        act.activation(kpe[:, kt, :], bank(b)[:, QR + KVR:BW], ACT.Copy)
                        if t == 0:
                            act.activation(ckv_out[:, :], bank(b)[:, QR:BW], ACT.Copy)
                        act.activation(st[:, 0:QR + KVR], bank(b)[:, 0:QR + KVR], ACT.Copy).then_inc(S["acc_copied"], 1)
                        if t == 0:
                            act.wait_ge(S["acc_copied"], n("acc_copied", 1))
                            act.dma_start(new_ckv[0, ds(layer, 1)].rearrange("l p d -> p (l d)"), ckv_out[:, 0:KVR])\
                               .then_inc(S["ctx_out"], 16)
                            act.dma_start(new_kpe[0, ds(layer, 1)].rearrange("l p d -> p (l d)"), ckv_out[:, KVR:])\
                               .then_inc(S["ctx_out"], 16)
                    elif kind == "bc":
                        act.activation(kpe[:, 1, :], cached[:, KVR:KVR + ROPE], ACT.Copy)
                        act.activation(st[:, QR:QR + KVR], cached[:, 0:KVR], ACT.Copy).then_inc(S["acc_copied"], 1)
                    elif it["q"]:
                        act.activation(st[:, 0:4 * QK], bank(b, 4 * QK), ACT.Copy).then_inc(S["acc_copied"], 1)
                    else:
                        heads = st[:, 0:4 * QK].rearrange("p (h d) -> p h d", h=4)
                        kv = bank(b).rearrange("p (h d) -> p h d", h=4)
                        act.activation(heads[:, :, 0:NOPE], kv[:, :, 0:NOPE], ACT.Copy)
                        act.activation(heads[:, :, NOPE:QK], kpe[:, t, :].unsqueeze(1).to_broadcast([P, 4, ROPE]), ACT.Copy)
                        act.activation(vB[:, t, :, :], kv[:, :, NOPE:], ACT.Copy).then_inc(S["acc_copied"], 1)

                def tick(s):
                    it = s["it"]
                    a, b = span(it)
                    act.wait_ge(S["acc_copied"], n("acc_copied", -s["acc_back"]))
                    act.wait_ge(S["ms_done"], n("ms_done", -s["sums_before"]))
                    act.activation(tmpq[:, it["par"], a:b], stage[:, it["slot"], a:b], ACT.Square).then_inc(S["sqr_done"], 1)

                def turn(s):
                    it = s["it"]
                    kind, t, k = it["kind"], it["tile"], key_tile(it)
                    act.wait_ge(S["t_done"], n("t_done", 1))
                    turned = bank(s["bank"]).rearrange("p (i c) -> p i c", c=P)
                    q, k = slice(t * P, (t + 1) * P), slice(k * P, (k + 1) * P)
                    if kind == "bq":
                        act.activation(bqT[:, :, q], turned[:, 0:2, :], ACT.Copy)
                        act.activation(ckvT[:, k], turned[:, 2, :], ACT.Copy).then_inc(S["t_copied"], 1)
                    else:
                        out = {"aq": lambda: qA[:, :, q], "ak": lambda: kA[:, :, k], "cq": lambda: qC[:, :, q],
                               "ck": lambda: kC[:, k], "bc": lambda: ckvT[:, k],
                               "up": lambda: (qB[0:QK, :, q] if it.get("q") else kB[0:QK, :, k])}[kind]()
                        src = {"ck": turned[:, 0, :], "bc": turned[:, 0, :], "up": turned[0:QK, :, :]}.get(kind, turned)
                        act.activation(out, src, ACT.Copy).then_inc(S["t_copied"], 1)
                    if t == 0 and kind == "ak":
                        act.dma_start(new_dk[0, ds(layer, 1)].rearrange("l p m h d -> p (l m h d)"), stage[:, it["slot"], :])\
                           .then_inc(S["ctx_out"], 16)
                    if t == 0 and kind == "ck":
                        act.dma_start(new_gk[0, ds(layer, 1)].rearrange("l p h d -> p (l h d)"), stage[:, it["slot"], 0:P])\
                           .then_inc(S["ctx_out"], 16)

                def turnc(s):
                    act.wait_ge(S["t_done"], n("t_done", 1))
                    if s["b"] == 0:
                        act.activation(kA[:, :, P:2 * P], bank(5).rearrange("p (i c) -> p i c", c=P), ACT.Copy)\
                           .then_inc(S["t_copied"], 1)
                    else:
                        act.activation(kC[:, P:2 * P], bank(5, P), ACT.Copy).then_inc(S["t_copied"], 1)

                def gate(s):
                    slot = s["g"] % GATE_SLOTS
                    act.wait_ge(S["sub_done"], n("sub_done", 1))
                    act.wait_ge(S["fm_read"], n("fm_read"))
                    act.wait_ge(S["mg_ready"], n("mg_ready"))
                    act.activation(gated[:, slot, :], run(3), ACT.Tanh, scale=0.5).then_inc(S["pair3_read"], 1)

                def score(s):
                    if s["first"]:
                        act.wait_ge(S["ctx_out"], n("ctx_out"))
                    act.wait_ge(S["max_ready"], n("max_ready", 1))
                    slot, pair = s["n"] % 4, s["n"] % 2
                    w = SEQ if s["q"] == 0 else T
                    act.activation(prob[:, slot, 0:w], run(pair, 0, w), ACT.Exp, bias=negmax[:, slot:slot + 1],
                                   accum_out=den[:, slot:slot + 1]).then_inc(S["exp_done"], 1)

                def turnp(s):
                    q = s["q"]
                    act.wait_ge(S["pt_done"], n("pt_done", 1))
                    act.wait_ge(S["av_done"], n("av_done"))
                    if q == 0:
                        act.activation(probTc[:, :], line(2, P), ACT.Copy).then_inc(S["pt_copied"], 1)
                    else:
                        act.activation(probT[:, :, (q - 1) * P:q * P], line(2).rearrange("p (k c) -> p k c", c=P), ACT.Copy)\
                           .then_inc(S["pt_copied"], 1)

                def cache(s):
                    act.wait_ge(S["olo_ready"], n("olo_ready"))
                    act.wait_ge(S["ohi_ready"], n("ohi_ready"))
                    act.wait_ge(S["av_done"], n("av_done"))
                    act.wait_ge(S["hlo_ready"], n("hlo_ready"))
                    one = ds(layer, 1)
                    if s["b"] == 0:
                        act.dma_start(cached[:, 0:512], cache_dk[0, one].rearrange("l p m h d -> p (l m h d)"))\
                           .then_inc(S["cache_loaded"], 16)
                        act.dma_start(vA[:, 1, :], cache_dv[0, one].rearrange("l p h d -> p (l h d)"))\
                           .then_inc(S["cache_loaded"], 16)
                    elif s["b"] == 1:
                        act.dma_start(cached[:, 0:KVR], cache_ckv[0, one].rearrange("l p d -> p (l d)"))\
                           .then_inc(S["cache_loaded"], 16)
                        act.dma_start(cached[:, KVR:KVR + ROPE], cache_kpe[0, one].rearrange("l p d -> p (l d)"))\
                           .then_inc(S["cache_loaded"], 16)
                    else:
                        act.dma_start(cached[:, 0:P], cache_gk[0, one].rearrange("l p h d -> p (l h d)"))\
                           .then_inc(S["cache_loaded"], 16)
                        act.dma_start(vC[:, 1, :], cache_gv[0, one].rearrange("l p h d -> p (l h d)"))\
                           .then_inc(S["cache_loaded"], 16)

                def osq(s):
                    act.wait_ge(S["pair3_read"], n("pair3_read"))
                    act.wait_ge(S["ostat_done"], n("ostat_done"))
                    act.activation(nsq[:, s["h"] % 2, :], oT[:, s["h"], :], ACT.Square).then_inc(S["osq_ready"], 1)

                def osplit(s):
                    act.wait_ge(S["pair3_read"], n("pair3_read"))
                    for k in range(4):
                        act.activation(ohi[:, k, :], oT[:, k, :], ACT.Copy).then_inc(S["ohi_ready"], 1)

                def msplit(s):
                    act.wait_ge(S["mg_ready"], n("mg_ready"))
                    for k in range(KD):
                        act.activation(hhi[:, k, :], merged[:, k, :], ACT.Copy, scale=0.5).then_inc(S["mhi_ready"], 1)

                def up_out(s):
                    u = n.turn * 2 + s["a"] + s["f0"]
                    act.wait_ge(S["sub_done"], n("sub_done"))
                    act.wait_ge(S["alo_ready"], n("alo_ready", -1))
                    for j, v in enumerate((va, vg)):
                        act.activation(v[:, s["s"], :], run(2 * s["s"] + j), ACT.Identity,
                                       scale=PT[:, ds(u + (P_W + 44 + j * FT), 1)], bias=PT[:, ds(u + (P_CB + j * FT), 1)])\
                           .then_inc(S["v_ready"], 1)

                def up_out2(s):
                    act.wait_ge(S["fm_read"], n("fm_read"))
                    act.activation(vg[:, s["s"], :], vg[:, s["s"], :], ACT.Silu).then_inc(S["silu_done"], 1)
                    act.wait_ge(S["prod_ready"], n("prod_ready", 1))
                    act.activation(ahi[:, ds(n.turn * 2 + s["a"], 1), :], va[:, s["s"], :].unsqueeze(1), ACT.Copy)\
                       .then_inc(S["ahi_ready"], 1)

                do = dict(params=params, norm=norm, wo_out=wo_out, down_out=down_out, apply=apply, split=split, acc=acc, tick=tick, turn=turn, turnc=turnc, gate=gate, score=score,
                          turnp=turnp, osq=osq, osplit=osplit, msplit=msplit, up_out=up_out,
                          up_out2=up_out2, cache=cache)
                walk(act, PLAN, do, lambda s: do[s["step"]](s), n)
            act.wait_ge(S["sq_added"], DEPTH * PER_LAYER["sq_added"] + CREDIT)
            for i in range(2 * NT):
                act.wait_ge(S["y_turned"], i + 1)
                act.activation(xin[:, i // 2, i % 2 * 512:(i % 2 + 1) * 512], bank(i % 4), ACT.Copy).then_inc(S["y_copied"], 1)

        @block.vector
        def _(dve):
            dve.wait_ge(S["const_set"], 4)
            dve.wait_ge(S["const_loaded"], 16 * 6)
            dve.wait_ge(S["ident_loaded"], 16)
            dve.wait_ge(S["c_ready"], 2)
            dve.tensor_tensor(csplit[:, :, 2:4], cT[:, :, :], csplit[:, :, 0:2].bitcast(F32), ALU.subtract).then_inc(S["c_ready"], 1)
            for k in range(1, KD):
                dve.wait_ge(S["x_squared"], k + 1)
                if k > 1:
                    dve.wait_ge(S["x_summed"], k - 1)
                dve.tensor_tensor(hf[:, 0, :], nsq[:, 0, :] if k == 1 else hf[:, 0, :], first_squares[k % 5], ALU.add)\
                   .then_inc(S["x_summed"], 1)
            with dve.Fori(0, DEPTH) as layer:
                n = Count(layer)

                def params(s):
                    dve.wait_ge(S["gains_loaded"], n("gains_loaded", 16 * 7))
                    for g, w, by in ((G_DQ, HD, HD ** -0.5), (G_GQ, HD, HD ** -0.5), (G_MQ, QK, QK ** -0.5)):
                        dve.tensor_scalar(gains[:, g:g + w], gains[:, g:g + w], by, None, ALU.mult).then_inc(S["gain_ready"], 1)
                    dve.tensor_tensor(lamv[:, 0, :], lamv[:, 0, :], lamv[:, 1, :], ALU.mult).then_inc(S["lam_step"], 1)
                    dve.tensor_tensor(lamv[:, 2, :], lamv[:, 2, :], lamv[:, 3, :], ALU.mult).then_inc(S["lam_step"], 1)
                    dve.wait_ge(S["lam_step"], n("lam_step", 2))
                    dve.tensor_reduce(lam2[:, :], lamv[:, 0:4:2, :], AX.X, ALU.add).then_inc(S["lam_step"], 1)
                    dve.wait_ge(S["lam_exp"], n("lam_exp", 1))
                    dve.scalar_tensor_tensor(out=neglam[:, :], in0=lame[:, 1:2], scalar=gains[:, G_LC:G_LC + 1],
                                             in1=lame[:, 0:1], op0=ALU.subtract, op1=ALU.subtract).then_inc(S["lam_step"], 1)
                    dve.wait_ge(S["par_ready"], n("par_ready", 1))
                    dve.tensor_tensor(dgain[:, :], PT[:, P_DN:P_DN + 1], gains[:, G_LC + 1:G_LC + 2], ALU.mult)\
                       .then_inc(S["lam_step"], 1)

                def diagonals(signal):
                    for t in range(NT):
                        dve.tensor_scalar(diag[:, t, :], ident[:, :], nrstd[:, t:t + 1], None, ALU.mult).then_inc(S[signal], 1)

                def modulation(s):
                    a, b = ((0, ADA_FIRST), (ADA_FIRST, 6 * KD))[s["part"]]
                    dve.wait_ge(S["ada_done"], n("ada_done"))
                    dve.tensor_tensor(mod[:, a:b, :], bank(6)[:, ADA_AT:ADA_AT + 2 * (b - a)].rearrange("p (t j) -> p t j", j=2),
                                      PT[:, a:b].unsqueeze(2).to_broadcast([P, b - a, 2]), ALU.add).then_inc(S["mod_ready"], 1)
                    dve.wait_ge(S["mod_ready"], n("mod_ready", 1))
                    g, t = ((P_NM, KD), (P_NF, 4 * KD))[s["part"]]
                    dve.scalar_tensor_tensor(out=scale[:, s["part"], :, :], in0=mod[:, t:t + KD, :], scalar=1.0,
                                             in1=PT[:, g:g + KD].unsqueeze(2).to_broadcast([P, KD, 2]),
                                             op0=ALU.add, op1=ALU.mult).then_inc(S["mod_ready"], 1)
                    dve.wait_ge(S["mod_ready"], n("mod_ready", 2))

                def ada_row(s):
                    dve.wait_ge(S["sub_done"], n("sub_done"))
                    dve.wait_ge(S["ada_done"], n("ada_done"))
                    dve.tensor_copy(ada_rows, bank(6)[0:4, 256:512]).then_inc(S["pair3_read"], 1)

                def norm(s):
                    dve.wait_ge(S["stat_done"], n("stat_done", 1))
                    dve.tensor_scalar(nmean[:, :], bank(6, NT), 1.0 / D, EPS, ALU.mult, ALU.add).then_inc(S["sums_read"], 1)
                    dve.wait_ge(S["nrs_ready"], n("nrs_ready", 1))
                    diagonals("diag_ready")

                def apply(s):
                    w = s["which"]
                    dve.wait_ge(S["bc_done"], n("bc_done"))
                    rows57 = ps[:, 4 * 512:8 * 512].rearrange("p (a c) -> p a c", a=2)[:, :, 512:512 + HALF]
                    for k in range(KD):
                        if k >= 4:
                            dve.wait_ge(S["hlo_ready"], n("hlo_ready", k - 3))
                        h = hf[:, k % 4, :]
                        dve.tensor_tensor(h.rearrange("p (a c) -> p a c", a=2), xT[:, k, :].rearrange("p (a c) -> p a c", a=2),
                                          rows57, ALU.mult).then_inc(S["xn_done"], 1)
                        dve.wait_ge(S["xn_done"], n("xn_done", k + 1))
                        for j, (a, b) in enumerate(((0, SEQ), (SEQ, T))):
                            ins = dve.tensor_scalar(h[:, a:b], h[:, a:b], scale[:, w, k, j:j + 1],
                                                    mod[:, 3 * KD * w + k, j:j + 1], ALU.mult, ALU.add)
                        ins.then_inc(S["hf_ready"], 1)

                def split(s):
                    dve.wait_ge(S["hi_ready"], n("hi_ready", 1))
                    src, dst = sub_views(s)
                    dve.tensor_tensor(dst(wlo), src, dst(whi).bitcast(F32), ALU.subtract).then_inc(S["lo_ready"], 1)

                to_norm, to_finish = [], []

                def finish():
                    if to_finish:
                        it, gained, cos, sin = to_finish.pop()
                        r0, half, x, cs, tc, ts = rope_views(it)
                        dve.wait_ge(S["gained"], gained)
                        dve.tensor_tensor(tc, x, cs[0], ALU.mult).then_inc(S["cos_done"], 1)
                        dve.wait_ge(S["cos_done"], cos)
                        dve.wait_ge(S["sin_ready"], sin)
                        dve.tensor_tensor(x, tc, ts, ALU.add).then_inc(S["item_ready"], 1)

                def apply_norm():
                    if to_norm:
                        it, at = to_norm.pop()
                        par, st = it["par"], stage[:, it["slot"], :]
                        dve.wait_ge(S["rstd_ready"], at["rstd_ready"])
                        h0 = 0
                        for c, nh, dh in it["groups"]:
                            x = st[:, c:c + nh * dh].rearrange("p (h d) -> p h d", h=nh)
                            ins = dve.tensor_tensor(x, x, rstd[:, par, h0:h0 + nh].unsqueeze(2).to_broadcast([P, nh, dh]), ALU.mult)
                            h0 += nh
                        ins.then_inc(S["xh_ready"], 1)
                        dve.wait_ge(S["xh_ready"], at["xh_ready"])
                        for g, (c, nh, dh) in zip(it["gains"], it["groups"]):
                            x = st[:, c:c + nh * dh].rearrange("p (h d) -> p h d", h=nh)
                            ins = dve.tensor_tensor(x, x, gains[:, g:g + dh].unsqueeze(1).to_broadcast([P, nh, dh]), ALU.mult)
                        ins.then_inc(S["gained" if it["rope"] else "item_ready"], 1)
                        if it["rope"]:
                            to_finish.append((it, at["gained"], at["cos_done"], at["sin_ready"]))

                def tick(s):
                    it = s["it"]
                    par = it["par"]
                    dve.wait_ge(S["sqr_done"], n("sqr_done", 1))
                    h0 = 0
                    for c, nh, dh in it["groups"]:
                        dve.tensor_reduce(ssum[:, par, h0:h0 + nh], tmpq[:, par, c:c + nh * dh].rearrange("p (h d) -> p h d", h=nh),
                                          AX.X, ALU.add).then_inc(S["ss_ready"], 1)
                        h0 += nh
                    dve.wait_ge(S["ss_ready"], n("ss_ready", len(it["groups"])))
                    h0 = 0
                    for c, nh, dh in it["groups"]:
                        dve.tensor_scalar(smean[:, par, h0:h0 + nh], ssum[:, par, h0:h0 + nh], 1.0 / dh, EPS,
                                          ALU.mult, ALU.add).then_inc(S["ms_done"], 1)
                        h0 += nh
                    finish()
                    apply_norm()
                    to_norm.append((it, {x: n(x, 1) for x in ("rstd_ready", "xh_ready", "gained", "cos_done", "sin_ready")}))

                def flush(s):
                    finish()
                    apply_norm()
                    finish()

                def score(s):
                    slot, pair = s["n"] % 4, s["n"] % 2
                    dve.wait_ge(S["score_done"], n("score_done", 1))
                    dve.tensor_reduce(negmax[:, slot:slot + 1], run(pair, 0, SEQ if s["q"] == 0 else T), AX.X, ALU.max,
                                      negate=True).then_inc(S["max_ready"], 1)

                def soft(s):
                    a = s["n"] % 4
                    w = SEQ if s["q"] == 0 else T
                    k = 2 if s["br"] == "A" else 1
                    dve.wait_ge(S["exp_done"], n("exp_done"))
                    dve.reciprocal(rden[:, a:a + k], den[:, a:a + k]).then_inc(S["rden_done"], 1)
                    dve.wait_ge(S["rden_done"], n("rden_done", 1))
                    if k == 1:
                        dve.tensor_scalar(prob[:, a, 0:w], prob[:, a, 0:w], rden[:, a:a + 1], None, ALU.mult)\
                           .then_inc(S["p_ready"], 1)
                    else:
                        dve.tensor_scalar(prob[:, a + 1, 0:w], prob[:, a + 1, 0:w], rden[:, a + 1:a + 2], neglam[:, 0:1],
                                          ALU.mult, ALU.mult).then_inc(S["p1_done"], 1)
                        dve.wait_ge(S["p1_done"], n("p1_done", 1))
                        dve.scalar_tensor_tensor(out=prob[:, a, 0:w], in0=prob[:, a, 0:w], scalar=rden[:, a:a + 1],
                                                 in1=prob[:, a + 1, 0:w], op0=ALU.mult, op1=ALU.add).then_inc(S["p_ready"], 1)

                def values(s):
                    h = s["h"]
                    dve.wait_ge(S["av_done"], n("av_done", 1))
                    p0, p1, tile = (0, P, h) if s["br"] == "A" else (h % 2 * 64, h % 2 * 64 + 64, h // 2)
                    dve.tensor_copy(oT[p0:p1, tile, :], line(3, T, p0, p1, off=512 - SEQ)).then_inc(S["pair3_read"], 1)

                def ostat(s):
                    dve.wait_ge(S["ostat_done"], n("ostat_done", 1))
                    dve.tensor_scalar(nmean[:, :], bank(6, NT), 1.0 / VD, EPS, ALU.mult, ALU.add).then_inc(S["sums_read"], 1)
                    dve.wait_ge(S["ors_ready"], n("ors_ready", 1))
                    diagonals("odiag_ready")

                def obcast(s):
                    dve.wait_ge(S["obc_done"], n("obc_done", 1))
                    dve.scalar_tensor_tensor(out=oT[:, s["h"], :], in0=oT[:, s["h"], :], scalar=dgain[:, 0:1], in1=run(3),
                                             op0=ALU.mult, op1=ALU.mult).then_inc(S["pair3_read"], 1)

                def osplit(s):
                    for k in range(4):
                        dve.wait_ge(S["ohi_ready"], n("ohi_ready", k + 1))
                        dve.tensor_tensor(olo[:, k, :], oT[:, k, :], ohi[:, k, :].bitcast(F32), ALU.subtract)\
                           .then_inc(S["olo_ready"], 1)

                def merge(s):
                    dve.wait_ge(S["sub_done"], n("sub_done"))
                    dve.wait_ge(S["pair3_read"], n("pair3_read"))
                    for j in range(2):
                        i = 2 * s["k"] + j
                        g = gated[:, i % GATE_SLOTS, :]
                        dve.scalar_tensor_tensor(out=g if s["b"] else merged[:, i, :], in0=g, scalar=1.0, in1=run(i % 3),
                                                 op0=ALU.add, op1=ALU.mult).then_inc(S["fm_read"], 1)

                def msplit(s):
                    for k in range(KD):
                        dve.wait_ge(S["mhi_ready"], n("mhi_ready", k + 1))
                        dve.scalar_tensor_tensor(out=hlo[:, k, :], in0=merged[:, k, :], scalar=0.5,
                                                 in1=hhi[:, k, :].bitcast(F32), op0=ALU.mult, op1=ALU.subtract)\
                           .then_inc(S["mlo_ready"], 1)

                def residual(f, pair, m0):
                    for j, (a, b) in enumerate(((0, SEQ), (SEQ, T))):
                        x = xT[:, ds(f, 1), a:b]
                        ins = dve.scalar_tensor_tensor(out=x, in0=run(pair, a, b).unsqueeze(1), scalar=mod[:, ds(f + m0, 1), j],
                                                       in1=x, op0=ALU.mult, op1=ALU.add)
                    ins.then_inc(S["fm_read"], 1)

                def zero(s):
                    if s["what"] == "wo":
                        dve.wait_ge(S["sub_done"], n("sub_done"))
                    dve.wait_ge(S["hhi_ready"], n("hhi_ready"))
                    dve.wait_ge(S["hlo_ready"], n("hlo_ready"))
                    dve.memset(hf[:, 0, :], 0.0).then_inc(S["zeroed"], 1)
                    dve.wait_ge(S["zeroed"], n("zeroed", 1))

                def add_squares(slots):
                    for j, slot in enumerate(slots):
                        dve.wait_ge(S["sq_ready"], n("sq_ready", j + 1 - len(slots)))
                        dve.wait_ge(S["sq_added"], n("sq_added", j))
                        dve.tensor_tensor(hf[:, 0, :], hf[:, 0, :], nsq[:, slot, :], ALU.add).then_inc(S["sq_added"], 1)

                def wo_out2(s):
                    add_squares((0, 1))

                def down_out2(s):
                    if s["squares"]:
                        add_squares((s["s"],))

                def wo_out(s):
                    dve.wait_ge(S["sub_done"], n("sub_done"))
                    for j in range(2):
                        residual((n.turn * 2 + s["a"]) * 2 + j, 2 * s["s"] + j, 2 * KD)

                def down_out(s):
                    dve.wait_ge(S["sub_done"], n("sub_done"))
                    residual(n.turn * 2 + s["a"], 2 * s["s"], 5 * KD)

                def up_out(s):
                    u = n.turn * 2 + s["a"] + s["f0"]
                    for j, v in enumerate((va, vg)):
                        v = v[:, s["s"], :]
                        pair = 2 * s["s"] + j
                        dve.wait_ge(S["v_ready"], n("v_ready", j + 1))
                        for a, b in ((0, SEQ), (SEQ, T)):
                            ins = dve.scalar_tensor_tensor(out=v[:, a + 1:b], in0=run(pair, a, b - 1),
                                                           scalar=PT[:, ds(u + (P_W + j * FT), 1)], in1=v[:, a + 1:b],
                                                           op0=ALU.mult, op1=ALU.add)
                        ins.then_inc(S["tap_done"], 1)
                        dve.wait_ge(S["tap_done"], n("tap_done", j + 1))
                        for a, b in ((0, SEQ), (SEQ, T)):
                            ins = dve.scalar_tensor_tensor(out=v[:, a:b - 1], in0=run(pair, a + 1, b),
                                                           scalar=PT[:, ds(u + (P_W + 88 + j * FT), 1)], in1=v[:, a:b - 1],
                                                           op0=ALU.mult, op1=ALU.add)
                        ins.then_inc(S["fm_read"], 1)

                do = dict(params=params, ada_row=ada_row, mod=modulation, norm=norm, apply=apply, split=split, tick=tick, flush=flush, score=score,
                          soft=soft, values=values, ostat=ostat, obcast=obcast, osplit=osplit, merge=merge,
                          msplit=msplit, zero=zero, wo_out=wo_out, wo_out2=wo_out2, down_out=down_out,
                          down_out2=down_out2, up_out=up_out)
                walk(dve, PLAN, do, lambda s: do[s["step"]](s), n)

        @block.gpsimd
        def _(pool):
            pool.memset(ones[:, :], 1.0).then_inc(S["const_set"], 1)
            pool.memset(mhalf[:, :], -0.5).then_inc(S["const_set"], 1)
            pool.memset(epsc[:, :], EPS).then_inc(S["const_set"], 1)
            for name in PER_LAYER:
                if name not in DMA_SEMS:
                    pool.sem_inc(S[name], CREDIT)
            pool.wait_ge(S["const_set"], 3)
            pool.memset(epsc[:, :], EPS).then_inc(S["const_set"], 1)
            pool.wait_ge(S["const_loaded"], 16 * 6)
            with pool.Fori(0, DEPTH) as layer:
                n = Count(layer)

                def norm(s):
                    pool.wait_ge(S["sums_read"], n("sums_read", 1))
                    pool.tensor_tensor(nrstd[:, :], nmean[:, :], mhalf[:, 0:NT], ALU.pow).then_inc(S["nrs_ready"], 1)

                def apply(s):
                    for k in range(KD):
                        pool.wait_ge(S["hhi_ready"], n("hhi_ready", k + 1))
                        pool.tensor_tensor(hlo[:, k, :], hf[:, k % 4, :], hhi[:, k, :].bitcast(F32), ALU.subtract)\
                            .then_inc(S["hlo_ready"], 1)

                to_turn = []

                def sine():
                    if to_turn:
                        it, gained, used = to_turn.pop()
                        pool.wait_ge(S["gained"], gained)
                        pool.wait_ge(S["item_ready"], used)
                        r0, half, x, cs, tc, ts = rope_views(it)
                        sn = cs[1]
                        pool.tensor_tensor(ts[:, :, 0:half], x[:, :, half:], sn[:, :, 0:half], ALU.mult)
                        pool.tensor_tensor(ts[:, :, half:], x[:, :, 0:half], sn[:, :, half:], ALU.mult).then_inc(S["sin_ready"], 1)

                def tick(s):
                    it = s["it"]
                    par, heads = it["par"], sum(g[1] for g in it["groups"])
                    pool.wait_ge(S["ms_done"], n("ms_done", len(it["groups"])))
                    pool.tensor_tensor(rstd[:, par, 0:heads], smean[:, par, 0:heads], mhalf[:, 0:heads], ALU.pow)\
                        .then_inc(S["rstd_ready"], 1)
                    sine()
                    if it["rope"]:
                        to_turn.append((it, n("gained", 1), n("item_ready")))

                def flush(s):
                    sine()

                def ostat(s):
                    pool.wait_ge(S["sums_read"], n("sums_read", 1))
                    pool.tensor_tensor(nrstd[:, :], nmean[:, :], mhalf[:, 0:NT], ALU.pow).then_inc(S["ors_ready"], 1)

                def merge(s):
                    if s["b"]:
                        for j in range(2):
                            i = 2 * s["k"] + j
                            pool.wait_ge(S["fm_read"], n("fm_read", j + 1))
                            pool.tensor_tensor(merged[:, i, :], merged[:, i, :], gated[:, i % GATE_SLOTS, :], ALU.add)\
                                .then_inc(S["mg_ready"], 1)

                def up_out2(s):
                    pool.wait_ge(S["silu_done"], n("silu_done", 1))
                    a = va[:, s["s"], :]
                    pool.tensor_tensor(a, a, vg[:, s["s"], :], ALU.mult).then_inc(S["prod_ready"], 1)
                    pool.wait_ge(S["ahi_ready"], n("ahi_ready", 1))
                    u = ds(n.turn * 2 + s["a"], 1)
                    pool.tensor_tensor(alo[:, u, :], a.unsqueeze(1), ahi[:, u, :].bitcast(F32), ALU.subtract)\
                        .then_inc(S["alo_ready"], 1)

                do = dict(norm=norm, apply=apply, tick=tick, flush=flush, ostat=ostat, merge=merge, up_out2=up_out2)
                walk(pool, PLAN, do, lambda s: do[s["step"]](s), n)


_INS = ["x_prompt", "x_sample", "c", "cache_diff_k", "cache_diff_v", "cache_mla_ckv", "cache_mla_kpe", "cache_gqa_k",
        "cache_gqa_v", "c_ctx", "w_ada", "b_ada", "norm_mix", "w_in", "diff_qk_norm", "diff_lambda", "diff_out_norm",
        "mla_q_norm", "w_mla_q_up", "mla_kv_norm", "w_mla_kv_up", "mla_qk_norm", "gqa_qk_norm", "w_branch_a",
        "w_branch_b", "w_branch_c", "w_o", "norm_ffn", "w_up", "conv_w", "conv_b", "w_down"]
_OUTS = [(1, SEQ, D), (1, DEC, D), (1, DEPTH, SEQ, 2, NH, HD), (1, DEPTH, SEQ, NH, VD), (1, DEPTH, SEQ, KVR),
         (1, DEPTH, SEQ, ROPE), (1, DEPTH, SEQ, GKV, HD), (1, DEPTH, SEQ, GKV, HD)]


def rope_table(dim):
    t = np.arange(DEC, dtype=np.float32)
    quarter = dim // 4
    inv = (np.float32(1.0) / np.float32(BASE) ** (np.arange(quarter, dtype=np.float32) / np.float32(quarter))).astype(np.float32)
    ang = np.concatenate([(t // GRID_W)[:, None] * inv, (t % GRID_W)[:, None] * inv], axis=-1).astype(np.float32)
    cos, sin = np.cos(ang), np.sin(ang)
    both = np.stack([np.concatenate([cos, cos], -1), np.concatenate([-sin, sin], -1)], 1).astype(np.float32)
    return np.ascontiguousarray(both.reshape(DEC // P, P, 2, dim).transpose(1, 0, 2, 3))


def layer_constants():
    lam = [0.8 - 0.6 * math.exp(-0.3 * layer) for layer in range(DEPTH)]
    return np.array([[x, 1.0 - x] for x in lam], dtype=np.float32)


def kernel(**inputs):
    import concourse.bacc as _bacc
    from concourse.bass_utils import run_bass_kernel_spmd as _run

    nc = _bacc.Bacc("TRN2", target_bir_lowering=False, num_devices=1)
    arrays, args = {}, []
    for name in _INS:
        arrays[f"in_{name}"] = np.ascontiguousarray(inputs[name])
    arrays["const_ident"] = np.eye(P, dtype=np.float32)
    arrays["const_rope_h"] = rope_table(HD)
    arrays["const_rope_r"] = rope_table(ROPE)
    arrays["const_layer"] = layer_constants()
    for name, a in arrays.items():
        args.append(nc.dram_tensor(name, a.shape, F32, kind="ExternalInput").ap())
    for i, shape in enumerate(_OUTS):
        args.append(nc.dram_tensor(f"out_{i}", shape, F32, kind="ExternalOutput").ap())
    program(nc, *args)
    r = _run(nc, [arrays], core_ids=[0])
    return tuple(r.results[0][f"out_{i}"] for i in range(len(_OUTS)))
```
